# Optimizing a Trainium2 kernel written in Bass

```python
import jax, jax.numpy as jnp
from jax import lax
import numpy as np

D_MODEL = 1024
BATCH = 1
SEQ = 256
DEPTH = 2
DEC_BATCH = 8
DEC_SEQ = 8
PAST_LEN = 2048
PAGE_SIZE = 128

MIX_WIDTH = D_MODEL
A_WIDTH = MIX_WIDTH // 2
B_WIDTH = MIX_WIDTH - A_WIDTH
CHUNK_A = 128
A_HEADS = 4
A_HEAD_DIM = A_WIDTH // A_HEADS
B_EXPAND = 128
B_HEADS = B_WIDTH // B_EXPAND
B_DK = B_EXPAND
B_DV = B_WIDTH // B_HEADS
B_QK = B_HEADS * B_DK
CHUNK_B = 64
IN_COLS = 2 * A_WIDTH + 2 * B_QK + 2 * B_WIDTH
SPLITS = [A_WIDTH, 2 * A_WIDTH, 2 * A_WIDTH + B_QK, 2 * A_WIDTH + 2 * B_QK, 2 * A_WIDTH + 2 * B_QK + B_WIDTH]
D_FF = 2816
N_EXPERTS = 8
TOP_K = 2
N_DENSE = (DEPTH + 1) // 2
N_MOE = DEPTH // 2
ALPHA = (2.0 * DEPTH) ** 0.25
BETA = (8.0 * DEPTH) ** -0.25
LN_EPS = 1e-5
RMS_EPS = 1e-6

kernel_name = "hymba_gmlp_hgrn2_deepnorm_adaln_moe_step"

def layer_norm(x, w, b):
    xf = x.astype(jnp.float32)
    mu = jnp.mean(xf, -1, keepdims=True)
    var = jnp.mean(jnp.square(xf - mu), -1, keepdims=True)
    return ((xf - mu) * lax.rsqrt(var + LN_EPS) * w.astype(jnp.float32) + b.astype(jnp.float32)).astype(x.dtype)

def chunk_spatial_gate(u, vn, w_s, b_s):
    bsz, t_len = u.shape[:2]
    n_chunks = -(-t_len // CHUNK_A)
    pad = n_chunks * CHUNK_A - t_len
    vp = jnp.pad(vn, ((0, 0), (0, pad), (0, 0), (0, 0))).reshape(bsz, n_chunks, CHUNK_A, A_HEADS, A_HEAD_DIM)
    causal = jnp.tril(jnp.ones((CHUNK_A, CHUNK_A), bool))
    w = jnp.where(causal[None], w_s, 0)
    mixed = jnp.einsum('hts,bcshd->bcthd', w, vp) + b_s.T[None, None, :, :, None]
    mixed = mixed.reshape(bsz, n_chunks * CHUNK_A, A_HEADS, A_HEAD_DIM)[:, :t_len]
    return u * mixed

def hgrn2_chunked(q, k, logf, v, s0):
    bsz, t_len = q.shape[:2]
    c_len = CHUNK_B if t_len >= CHUNK_B else t_len
    n_chunks = -(-t_len // c_len)
    pad = n_chunks * c_len - t_len

    def prep(a):
        a = jnp.pad(a, ((0, 0), (0, pad), (0, 0), (0, 0)))
        return a.reshape(bsz, n_chunks, c_len, a.shape[2], a.shape[3]).transpose(1, 0, 3, 2, 4)

    qc, kc, gc, vc = prep(q), prep(k), prep(logf), prep(v)
    causal = jnp.tril(jnp.ones((c_len, c_len), bool))[:, :, None]

    def step(s, xs):
        qb, kb, gb, vb = xs
        bcum = jnp.cumsum(gb, axis=2)
        diff = bcum[:, :, :, None, :] - bcum[:, :, None, :, :]
        decay = jnp.exp(jnp.where(causal, diff, -jnp.inf))
        scores = jnp.einsum('bhtd,bhsd,bhtsd->bhts', qb, kb, decay)
        o = jnp.einsum('bhts,bhsv->bhtv', scores, vb) + jnp.einsum('bhtd,bhdv->bhtv', qb * jnp.exp(bcum), s)
        blast = bcum[:, :, -1:, :]
        s_new = jnp.exp(blast[:, :, 0, :])[..., None] * s + jnp.einsum('bhsd,bhsv->bhdv', kb * jnp.exp(blast - bcum), vb)
        return s_new, o

    s_fin, o = lax.scan(step, s0, (qc, kc, gc, vc))
    o = o.transpose(1, 0, 3, 2, 4).reshape(bsz, n_chunks * c_len, q.shape[2], v.shape[3])[:, :t_len]
    return o, s_fin

def token_mixer(h, s0, w_in, w_out, a_ln_w, a_ln_b, a_ws, a_bs, lb, b_norm_w):
    bsz, t_len, _ = h.shape
    proj = jnp.einsum('btd,de->bte', h, w_in)
    u, v, q, f, i, g = jnp.split(proj, SPLITS, axis=-1)
    u = jax.nn.gelu(u, approximate=False)
    vn = layer_norm(jax.nn.gelu(v, approximate=False), a_ln_w, a_ln_b)
    a_out = chunk_spatial_gate(u.reshape(bsz, t_len, A_HEADS, A_HEAD_DIM),
                               vn.reshape(bsz, t_len, A_HEADS, A_HEAD_DIM), a_ws, a_bs).reshape(bsz, t_len, A_WIDTH)
    lbh = lb.reshape(B_HEADS, B_DK)
    fg = lbh + (1.0 - lbh) * jax.nn.sigmoid(f.astype(jnp.float32).reshape(bsz, t_len, B_HEADS, B_DK))
    qq = jax.nn.silu(q.astype(jnp.float32)).reshape(bsz, t_len, B_HEADS, B_DK)
    ii = i.astype(jnp.float32).reshape(bsz, t_len, B_HEADS, B_DV)
    o, s_new = hgrn2_chunked(qq, 1.0 - fg, jnp.log(fg), ii, s0.astype(jnp.float32))
    o = o * lax.rsqrt(jnp.mean(o * o, -1, keepdims=True) + RMS_EPS) * b_norm_w.astype(jnp.float32)
    b_out = o.reshape(bsz, t_len, B_WIDTH) * jax.nn.silu(g.astype(jnp.float32))
    mix = jnp.concatenate([a_out, b_out.astype(h.dtype)], axis=-1)
    y = jnp.einsum('bte,ed->btd', mix, w_out)
    start = CHUNK_A * ((t_len - 1) // CHUNK_A)
    return y, s_new.astype(s0.dtype), vn[:, start:]

def swiglu(h, wg, wu, wd):
    return jnp.einsum('btf,fd->btd', jax.nn.silu(jnp.einsum('btd,df->btf', h, wg)) * jnp.einsum('btd,df->btf', h, wu), wd)

def moe_swiglu(h, w_router, e_gate, e_up, e_down):
    probs = jax.nn.softmax(jnp.einsum('btd,de->bte', h, w_router).astype(jnp.float32), axis=-1)
    top_v, top_i = lax.top_k(probs, TOP_K)
    top_v = top_v / jnp.sum(top_v, -1, keepdims=True)
    combine = jnp.sum(jax.nn.one_hot(top_i, N_EXPERTS, dtype=jnp.float32) * top_v[..., None], axis=-2)
    y = jnp.zeros_like(h)
    for e in range(N_EXPERTS):
        y = y + combine[..., e:e + 1].astype(h.dtype) * swiglu(h, e_gate[e], e_up[e], e_down[e])
    return y

def trunk(x, c, s_all, w_ada, b_ada, w_in, w_out, a_ln_w, a_ln_b, a_ws, a_bs, lb_all, b_norm_w,
          ln1_w, ln1_b, ln2_w, ln2_b, w_ff_gate, w_ff_up, w_ff_down, w_router, e_gate, e_up, e_down):
    c_act = jax.nn.silu(c)
    states, vrows = [], []
    for l in range(DEPTH):
        mod = jnp.einsum('bd,de->be', c_act, w_ada[l]) + b_ada[l]
        sh1, sc1, gt1, sh2, sc2, gt2 = [m[:, None, :] for m in jnp.split(mod, 6, axis=-1)]
        h = x * (1.0 + sc1) + sh1
        y, s_new, vn = token_mixer(h, s_all[l], w_in[l], w_out[l], a_ln_w[l], a_ln_b[l], a_ws[l], a_bs[l],
                                   lb_all[l], b_norm_w[l])
        x = layer_norm(ALPHA * x + gt1 * y, ln1_w[l], ln1_b[l])
        h = x * (1.0 + sc2) + sh2
        if l % 2 == 0:
            f_out = swiglu(h, w_ff_gate[l // 2], w_ff_up[l // 2], w_ff_down[l // 2])
        else:
            f_out = moe_swiglu(h, w_router[l // 2], e_gate[l // 2], e_up[l // 2], e_down[l // 2])
        x = layer_norm(ALPHA * x + gt2 * f_out, ln2_w[l], ln2_b[l])
        states.append(s_new)
        vrows.append(vn)
    return x, jnp.stack(states, axis=0), jnp.stack(vrows, axis=0)

def setup_inputs(seed: int = 0) -> dict:
    key = jax.random.key(seed)
    ks = jax.random.split(key, 32)

    def nrm(k, shape, scale):
        return jax.random.normal(k, shape, jnp.float32) * scale

    d = D_MODEL
    gate_offset = jnp.concatenate([jnp.zeros((2 * d,), jnp.float32), jnp.ones((d,), jnp.float32),
                                   jnp.zeros((2 * d,), jnp.float32), jnp.ones((d,), jnp.float32)])
    return {
        'x_prompt': nrm(ks[0], (BATCH, SEQ, d), 1.0),
        'x_sample': nrm(ks[1], (DEC_BATCH, DEC_SEQ, d), 1.0),
        'state_hgrn': nrm(ks[2], (DEPTH, DEC_BATCH, B_HEADS, B_DK, B_DV), 0.5),
        'c_prompt': nrm(ks[3], (BATCH, d), 1.0),
        'c_sample': nrm(ks[4], (DEC_BATCH, d), 1.0),
        'w_ada': nrm(ks[5], (DEPTH, d, 6 * d), 0.2 * d ** -0.5),
        'b_ada': nrm(ks[6], (DEPTH, 6 * d), 0.02) + gate_offset,
        'w_in': nrm(ks[7], (DEPTH, d, IN_COLS), d ** -0.5),
        'w_out': nrm(ks[8], (DEPTH, MIX_WIDTH, d), BETA * MIX_WIDTH ** -0.5),
        'a_ln_w': 1.0 + nrm(ks[9], (DEPTH, A_WIDTH), 0.02),
        'a_ln_b': nrm(ks[10], (DEPTH, A_WIDTH), 0.02),
        'a_ws': nrm(ks[11], (DEPTH, A_HEADS, CHUNK_A, CHUNK_A), CHUNK_A ** -0.5),
        'a_bs': 1.0 + nrm(ks[12], (DEPTH, A_HEADS, CHUNK_A), 0.02),
        'lb_logits': nrm(ks[13], (DEPTH, B_QK), 0.5),
        'b_norm_w': 1.0 + nrm(ks[14], (DEPTH, B_DV), 0.02),
        'ln1_w': 1.0 + nrm(ks[15], (DEPTH, d), 0.02),
        'ln1_b': nrm(ks[16], (DEPTH, d), 0.02),
        'ln2_w': 1.0 + nrm(ks[17], (DEPTH, d), 0.02),
        'ln2_b': nrm(ks[18], (DEPTH, d), 0.02),
        'w_ff_gate': nrm(ks[19], (N_DENSE, d, D_FF), d ** -0.5),
        'w_ff_up': nrm(ks[20], (N_DENSE, d, D_FF), d ** -0.5),
        'w_ff_down': nrm(ks[21], (N_DENSE, D_FF, d), BETA * D_FF ** -0.5),
        'w_router': nrm(ks[22], (N_MOE, d, N_EXPERTS), d ** -0.5),
        'e_gate': nrm(ks[23], (N_MOE, N_EXPERTS, d, D_FF), d ** -0.5),
        'e_up': nrm(ks[24], (N_MOE, N_EXPERTS, d, D_FF), d ** -0.5),
        'e_down': nrm(ks[25], (N_MOE, N_EXPERTS, D_FF, d), BETA * D_FF ** -0.5),
    }

def reference(x_prompt, x_sample, state_hgrn, c_prompt, c_sample, w_ada, b_ada, w_in, w_out, a_ln_w, a_ln_b,
              a_ws, a_bs, lb_logits, b_norm_w, ln1_w, ln1_b, ln2_w, ln2_b, w_ff_gate, w_ff_up, w_ff_down,
              w_router, e_gate, e_up, e_down):
    p = jax.nn.softmax(lb_logits.astype(jnp.float32), axis=0)
    lb_all = jnp.cumsum(p, axis=0) - p[0:1]
    weights = (w_ada, b_ada, w_in, w_out, a_ln_w, a_ln_b, a_ws, a_bs, lb_all, b_norm_w,
               ln1_w, ln1_b, ln2_w, ln2_b, w_ff_gate, w_ff_up, w_ff_down, w_router, e_gate, e_up, e_down)
    s_prompt0 = jnp.zeros((DEPTH, x_prompt.shape[0], B_HEADS, B_DK, B_DV), state_hgrn.dtype)
    y_prompt, state_hgrn_prompt, chunkv_prompt = trunk(x_prompt, c_prompt, s_prompt0, *weights)
    y_sample, state_hgrn_sample, chunkv_sample = trunk(x_sample, c_sample, state_hgrn, *weights)
    return (y_prompt, y_sample, state_hgrn_prompt, state_hgrn_sample, chunkv_prompt, chunkv_sample)


_drawn_inputs = setup_inputs


def setup_inputs(seed=0):
    import zlib

    import numpy as np

    out = dict(_drawn_inputs(seed))
    spreads = {}
    factors = {'a_ln_w': 8.018, 'a_ln_b': 8.204, 'a_bs': 4.836, 'b_norm_w': 6.038}
    for name, (base, spread) in spreads.items():
        noise = np.random.default_rng([zlib.crc32(name.encode()), seed]).standard_normal(out[name].shape)
        drawn = base * np.exp(spread * noise) if base else spread * noise
        out[name] = __import__('jax').numpy.asarray(drawn.astype(out[name].dtype))
    for name, factor in factors.items():
        out[name] = (out[name] * factor).astype(out[name].dtype)
    return out
```

```python
from contextlib import ExitStack

import concourse.bass as bass
from concourse import mybir

ALU = mybir.AluOpType
ACT = mybir.ActivationFunctionType
AX = mybir.AxisListType
F32 = mybir.dt.float32
F32R = mybir.dt.float32r
I32 = mybir.dt.int32

P = 128


class Signal:

    def __init__(self, sem, per=1, base=0):
        self.sem, self.per, self.base = sem, per, base

    def at(self, turn, i=0):
        return turn * self.per + (self.base + i + 1)


def hybrid_trunk(nc, x_prompt, x_sample, state_hgrn, c_prompt, c_sample, w_ada, b_ada, w_in, w_out,
                 a_ln_w, a_ln_b, a_ws, a_bs, lb_logits, b_norm_w, ln1_w, ln1_b, ln2_w, ln2_b,
                 w_ff_gate, w_ff_up, w_ff_down, w_router, e_gate, e_up, e_down,
                 y_prompt, y_sample, st_prompt, st_sample, chunkv_prompt, chunkv_sample):
    D = x_prompt.shape[2]
    TP = x_prompt.shape[1]
    NB, DS = x_sample.shape[0], x_sample.shape[1]
    TS = NB * DS
    T = TP + TS
    DEPTH = w_ada.shape[0]
    KD = D // P
    H = a_ws.shape[1]
    AW = H * P
    NE = w_router.shape[2]
    DFF = w_ff_gate.shape[2]
    ALPHA = (2.0 * DEPTH) ** 0.25
    LN_EPS, RMS_EPS = 1e-5, 1e-6
    NM = 6 * KD
    NC = 1 + NB
    TILES = [(0, P), (P, P), (TP, TS)]
    NT = len(TILES)
    CW = 256
    SLOT = KD * CW
    NFC = DFF // CW
    LEVELS = [64, 32, 16, 8, 4, 2, 1]
    NL = len(LEVELS) + 1
    assert TP == 2 * P and D == NFC * 0 + KD * P and DEPTH == 2 and DFF % CW == 0 and DS == 8

    WIN_ORDER = [6, 7, 4, 5, 8, 9, 2, 3, 0, 1, 10, 11]
    ADA_A = 2 * KD * P // CW
    NADA = 6 * D // CW
    NWIN = len(WIN_ORDER)
    NWO = D // CW
    RAW, SPL = 4, 3
    FFN_ORDER = [("gate", 0), ("up", 0)]
    for c in range(1, NFC):
        FFN_ORDER += [("gate", c), ("down", c - 1), ("up", c)]
    FFN_ORDER += [("down", NFC - 1)]
    MOE_ORDER = [("gate", 0), ("up", 0)]
    for c in range(1, NFC):
        MOE_ORDER += [("gate", c), ("up", c), ("down", c - 1)]
    MOE_ORDER += [("down", NFC - 1)]
    NMC = len(MOE_ORDER)

    stream = [("ada", 0, c) for c in range(ADA_A)]
    fill = [("ada", 0, c) for c in range(ADA_A, NADA)]
    for c in WIN_ORDER:
        stream += [("win", 0, c)] + [fill.pop(0)]
    stream += fill + [("ada", 1, c) for c in range(NADA)]
    stream += [("wout", 0, c) for c in range(NWO)]
    stream += [(k, 0, c) for k, c in FFN_ORDER]
    stream += [("win", 1, c) for c in WIN_ORDER] + [("wout", 1, c) for c in range(NWO)]
    split_index, ada_index, place = {}, {}, {}
    for n, key in enumerate(stream):
        place[key] = n % RAW
        if key[0] == "ada":
            ada_index[key] = len(ada_index)
        else:
            split_index[key] = len(split_index)
    NSPLIT = len(split_index)
    SKIP = -NMC % RAW
    SKIP_AT = [NMC * (i + 1) // (SKIP + 1) for i in range(SKIP)]
    assert NMC % SPL == 0
    MOE_RAW0 = len(stream)

    with ExitStack() as ctx:
        def sb(name, shape, dt=F32, c=ctx):
            return c.enter_context(nc.sbuf_tensor(name, shape, dt))

        def signal(name, per=1, base=0):
            return Signal(ctx.enter_context(nc.semaphore(name)), per, base)

        raw = sb("raw_ring", [P, RAW, SLOT])
        w_hi = sb("w_hi", [P, SPL, SLOT], F32R)
        w_lo = sb("w_lo", [P, SPL, SLOT], F32R)
        xT = sb("xT", [P, KD, T])
        act_hi = sb("act_hi", [P, KD, T], F32R)
        act_lo = sb("act_lo", [P, KD, T], F32R)
        ident = sb("ident", [P, P])
        ones = sb("ones", [P, P])
        before = sb("before", [P, P])
        lvl_mask = sb("lvl_mask", [P, NL - 1, P])
        keep = sb("keep", [P, T])
        col_iota = sb("col_iota", [P, P])
        rep8 = sb("rep8", [DS, TS])
        same_seq = sb("same_seq", [TS, TS])
        in_seq = sb("in_seq", [TS, NB])
        lower_e = sb("lower_e", [P, NE, NE])
        eps = sb("eps", [P, 2])
        cT = sb("cT", [P, KD, NC])
        NV = NM + 4 * KD + H + 1
        vecT = sb("vecT", [P, DEPTH, NV])
        lbv = sb("lbv", [P, DEPTH, 2, H])
        modT = sb("modT", [P, NM, NC])
        nmean = sb("nmean", [P, T])
        w_rt = sb("w_rt", [P, KD, NE])

        V_ADA, V_LN1W, V_LN1B, V_LN2W, V_LN2B = 0, NM, NM + KD, NM + 2 * KD, NM + 3 * KD
        V_LB, V_BN = NM + 4 * KD, NM + 4 * KD + H

        with ExitStack() as c1:
            vtok = sb("vtok", [P, NT, AW], c=c1)
            itok = sb("itok", [P, NT, AW], c=c1)
            ug = sb("ug", [P, 2 * H, T], c=c1)
            q = sb("q", [P, H, T], c=c1)
            k = sb("k", [P, H, T], c=c1)
            fe = sb("fe", [P, H, T], c=c1)
            bc = sb("bc", [P, H, T], c=c1)
            ze = sb("ze", [P, 2, H, T], c=c1)
            S = sb("S", [P, H, T], c=c1)
            kd = sb("kd", [P, NT, AW], c=c1)
            st = sb("st", [P, 2, NB, P], c=c1)
            stp = sb("stp", [P, H, P], c=c1)
            lnwb = sb("lnwb", [P, 2, AW], c=c1)
            lnw, lnb = lnwb[:, 0, :], lnwb[:, 1, :]
            iexp = lnwb[0:TS].rearrange("p a n -> p (a n)").rearrange("p (b v) -> p b v", v=P)
            ws = sb("ws", [P, H, P], c=c1)
            wsT = sb("wsT", [P, H, P], c=c1)
            wsS = sb("wsS", [TS, H, TS], c=c1)
            bsr = sb("bsr", [1, H, P], c=c1)
            vstat = sb("vstat", [P, NT, 6], c=c1)
            vmv = sb("vmv", [P, NT, 4], c=c1)
            hmix = ze[:].rearrange("p a h t -> p (a h) t")
            D_, Z = ze[:, 0], ze[:, 1]
        with ExitStack() as c2:
            hf = sb("hf", [P, KD, T], c=c2)
            accT = sb("accT", [P, KD, T], c=c2)
            tok_hi = sb("tok_hi", [P, NT, D], F32R, c=c2)
            tok_lo = sb("tok_lo", [P, NT, D], F32R, c=c2)
            G = sb("G", [P, NT, NE, P], F32R, c=c2)
            GT = sb("GT", [P, NE, T], F32R, c=c2)
            y_hi = sb("y_hi", [P, D], F32R, c=c2)
            y_lo = sb("y_lo", [P, D], F32R, c=c2)
            sil = sb("sil", [P, 2 * T], c=c2)
            aa = sb("aa", [P, 2 * T], c=c2)
            lg = sb("lg", [P, 8, NT, NE], c=c2)
            cmp = sb("cmp", [P, 2, NT, NE, NE], c=c2)
            red = sb("red", [P, 8, NT], c=c2)
            wslot = sb("wslot", [P, NE], c=c2)
            cnt = sb("cnt", [P, 16], c=c2)
            rounds_i = sb("rounds_i", [P, 1], I32, c=c2)
            yf = hf[:, 0:4, :].rearrange("p k t -> p (k t)")[:, 0:D]
            xg_hi, xg_lo = (a[:].rearrange("p k t -> p (k t)")[:, 0:KD * P].rearrange("p (k t) -> p k t", k=KD)
                            for a in (act_hi, act_lo))
            aT_hi, aT_lo = (a[:].rearrange("p k t -> p (k t)")[:, KD * P:KD * P + 2 * P]
                            .rearrange("p (k t) -> p k t", k=2) for a in (act_hi, act_lo))
            dT_hi, dT_lo = (a[:, 0:2 * T].rearrange("p (j t) -> p j t", t=T) for a in (y_hi, y_lo))
        with ExitStack() as c3:
            xtok = sb("xtok", [P, NT, D], c=c3)
            crow = sb("crow", [NC, D], c=c3)
            vrow = sb("vrow", [NV, DEPTH, P], c=c3)
            lt = sb("lt", [P, 8, H], c=c3)
        bank = [ctx.enter_context(nc.psum_tensor(f"bank{i}", [P, 512], F32)) for i in range(8)]

        rows_in = signal("rows_in")
        prep_in = signal("prep_in")
        consts = signal("consts")
        crow_silu = signal("crow_silu")
        first_T = signal("first_T")
        first_read = signal("first_read")
        vec_ready = signal("vec_ready")
        lt_exp = signal("lt_exp")
        raw_in = [signal(f"raw_in{i}") for i in range(RAW)]
        hi_ready = signal("hi_ready")
        lo_ready = signal("lo_ready")
        ada_used = signal("ada_used")
        ada_row = signal("ada_row")
        ada_T = signal("ada_T")
        mod_read = signal("mod_read", 2)
        dve_link = signal("dve_link")
        act_link = signal("act_link")
        pool_link = signal("pool_link")
        h_ready = signal("h_ready", 4)
        h_hi = signal("h_hi", 4)
        h_lo = signal("h_lo", 4)
        ws_T = signal("ws_T", 2)
        ws_read = signal("ws_read", 2)
        ws_masked = signal("ws_masked")
        NEV = 4 * H + 4 * NT
        proj = signal("proj", NEV)
        proj_read = signal("proj_read", NEV)
        fg_ready = signal("fg_ready")
        lf_ready = signal("lf_ready")
        bc_ready = signal("bc_ready")
        eb_ready = signal("eb_ready")
        D_ready = signal("D_ready", NL)
        E_ready = signal("E_ready", NL)
        Z_ready = signal("Z_ready", NL - 1)
        lvl_done = signal("lvl_done", NL)
        P_read = signal("P_read", NL)
        v_var = signal("v_var")
        v_sd = signal("v_sd")
        vn_ready = signal("vn_ready")
        qk_ready = signal("qk_ready")
        kd_T = signal("kd_T", NT)
        kd_ready = signal("kd_ready", NT)
        sp_mm = signal("sp_mm", 2)
        sp_ready = signal("sp_ready", 2)
        st_in = [signal(f"st_in{i}", H // 2) for i in range(2)]
        st_out = [signal(f"st_out{i}", H // 2) for i in range(2)]
        io_out = signal("io_out")
        ix_ready = signal("ix_ready", H)
        o_mm = signal("o_mm", H)
        o_ready = signal("o_ready", H)
        su_mm = signal("su_mm", H)
        st_new = signal("st_new", H)
        ms_mm = signal("ms_mm", H)
        rs_ready = signal("rs_ready", H)
        b_ready = signal("b_ready")
        mx_mm = signal("mx_mm", NT)
        mx_read = signal("mx_read", NT)
        mix_hi = signal("mix_hi", 2)
        mix_lo = signal("mix_lo", 2)
        wo_mm = signal("wo_mm", KD)
        wo_read = signal("wo_read", KD)
        z_ready = signal("z_ready", 2)
        mean_mm = signal("mean_mm", 2)
        mean_ready = signal("mean_ready", 2)
        zc_ready = signal("zc_ready", 4)
        sq_ready = signal("sq_ready", 4)
        var_mm = signal("var_mm", 2)
        sd_ready = signal("sd_ready", 2)
        x_ready = signal("x_ready", 2)
        g_mm = signal("g_mm", 2)
        g_read = signal("g_read", 2)
        u_mm = signal("u_mm", 2)
        a_ready = signal("a_ready", 2)
        a_hi = signal("a_hi")
        a_lo = signal("a_lo")
        d_mm = signal("d_mm", KD)
        d_read = signal("d_read", KD)
        rt_mm = signal("rt_mm")
        rt_sub = signal("rt_sub")
        rt_exp = signal("rt_exp")
        sel_ready = signal("sel_ready")
        pos_mm = signal("pos_mm")
        rounds_ready = signal("rounds_ready")
        h2_T = signal("h2_T")
        h2_hi = signal("h2_hi")
        h2_lo = signal("h2_lo")
        G_ready = signal("G_ready")
        GT_mm = signal("GT_mm", NE)
        GT_read = signal("GT_read", NE)
        wsl_mm = signal("wsl_mm")
        wsl_ready = signal("wsl_ready")
        gx_mm = signal("gx_mm", 2)
        xg_hi_ready = signal("xg_hi_ready", 2)
        xg_lo_ready = signal("xg_lo_ready", 2)
        eg_mm = signal("eg_mm", NFC)
        eg_read = signal("eg_read", NFC)
        eu_mm = signal("eu_mm", NFC)
        ea_ready = signal("ea_ready", NFC)
        eT_mm = signal("eT_mm", NFC)
        ea_hi = signal("ea_hi", NFC)
        ea_lo = signal("ea_lo", NFC)
        ed_mm = signal("ed_mm", NFC)
        y_read = signal("y_read", 2)
        yw_hi = signal("yw_hi", 2)
        yw_lo = signal("yw_lo", 2)
        sc_mm = signal("sc_mm", KD)
        sc_read = signal("sc_read", KD, base=1)
        out_T = signal("out_T", 2)
        out_read = signal("out_read", 2)
        outs = signal("outs")

        block = ctx.enter_context(nc.Block())

        def tiled(ap):
            return ap.rearrange("(k p) n -> p k n", p=P)

        def chunk_source(kind, l, c):
            if kind == "ada":
                return tiled(w_ada[l])[:, :, c * CW:(c + 1) * CW]
            if kind == "win":
                return tiled(w_in[l])[:, :, c * CW:(c + 1) * CW]
            if kind == "wout":
                return tiled(w_out[l])[:, :, c * CW:(c + 1) * CW]
            if kind == "gate":
                return tiled(w_ff_gate[0])[:, :, c * CW:(c + 1) * CW]
            if kind == "up":
                return tiled(w_ff_up[0])[:, :, c * CW:(c + 1) * CW]
            return tiled(w_ff_down[0])[:, 2 * c:2 * c + 2, :]

        def slot_as(buf, s, kind):
            if kind == "down":
                return buf[:, s, :].rearrange("p (j n) -> p j n", n=D)
            return buf[:, s, :].rearrange("p (k n) -> p k n", n=CW)

        def moe_raw(j):
            slot = lambda i: (MOE_RAW0 + i + sum(i >= at for at in SKIP_AT)) % RAW
            s = slot(j)
            use = sum(1 for i in range(j) if slot(i) == s)
            per = sum(1 for i in range(NMC) if slot(i) == s)
            return s, use, per

        RAW_USES = [sum(1 for n in range(MOE_RAW0) if n % RAW == s) for s in range(RAW)]

        @block.sync
        def _(sp):
            for l in range(DEPTH):
                for src, r0 in ((b_ada, V_ADA), (ln1_w, V_LN1W), (ln1_b, V_LN1B), (ln2_w, V_LN2W),
                                (ln2_b, V_LN2B), (lb_logits, V_LB), (b_norm_w, V_BN)):
                    n = src.shape[1] // P
                    sp.dma_start(vrow[r0:r0 + n, l, :], src[l].rearrange("(r p) -> r p", p=P)).then_inc(rows_in.sem, 16)
            sp.dma_start(crow[0:1, :], c_prompt).then_inc(rows_in.sem, 16)
            sp.dma_start(crow[1:NC, :], c_sample).then_inc(rows_in.sem, 16)
            sp.dma_start(xtok[:, 0:2, :], x_prompt[0].rearrange("(t p) d -> p t d", p=P)).then_inc(rows_in.sem, 16)
            sp.dma_start(xtok[0:TS, 2, :], x_sample.rearrange("b s d -> (b s) d")).then_inc(rows_in.sem, 16)
            sp.dma_start(w_rt[:], tiled(w_router[0])).then_inc(rows_in.sem, 16)
            for n, key in enumerate(stream):
                if n >= RAW:
                    old = stream[n - RAW]
                    if old[0] == "ada":
                        sp.wait_ge(ada_used.sem, ada_index[old] + 1)
                    else:
                        sp.wait_ge(lo_ready.sem, split_index[old] + 1)
                sp.dma_start(slot_as(raw, n % RAW, key[0]), chunk_source(*key)).then_inc(raw_in[n % RAW].sem, 16)
            sp.wait_ge(rounds_ready.sem, 1)
            rounds = sp.value_load(rounds_i[0:1, 0:1], min_val=1, max_val=NT)
            with sp.Fori(0, rounds) as rd:
                with sp.Fori(0, NE) as e:
                    it = sp.snap(rd * NE + e)
                    for j, (kind, c) in enumerate(MOE_ORDER):
                        s, _, _ = moe_raw(j)
                        old = max([i for i in range(j) if moe_raw(i)[0] == s], default=j - RAW)
                        sp.wait_ge(lo_ready.sem, it * NMC + (NSPLIT + old + 1))
                        w = {"gate": e_gate, "up": e_up, "down": e_down}[kind][0]
                        w = w[bass.ds(e, 1)].rearrange("o (k p) n -> p (o k) n", p=P)
                        w = w[:, 2 * c:2 * c + 2, :] if kind == "down" else w[:, :, c * CW:(c + 1) * CW]
                        sp.dma_start(slot_as(raw, s, kind), w).then_inc(raw_in[s].sem, 16)
            for t, (t0, n) in enumerate(TILES):
                sp.wait_ge(out_read.sem, 2 * t + 2)
                dst = y_prompt[0, t0:t0 + n, :] if t < 2 else y_sample.rearrange("b s d -> (b s) d")
                sp.dma_start(dst, xtok[0:n, t, :]).then_inc(outs.sem, 16)
            sp.wait_ge(outs.sem, 16 * NT)

        @block.gpsimd
        def _(pool):
            count = [0]

            def link(ins):
                count[0] += 1
                ins.then_inc(pool_link.sem, 1)
                pool.wait_ge(pool_link.sem, count[0])

            link(pool.memset(ident[:], 0.0))
            link(pool.affine_select(out=ident[:], in_=ident[:], compare_op=ALU.not_equal, fill=1.0, base=0,
                                    pattern=[[-1, P]], channel_multiplier=1))
            link(pool.memset(ones[:], 1.0))
            link(pool.affine_select(out=before[:], in_=ones[:], compare_op=ALU.is_ge, fill=0.0, base=-1,
                                    pattern=[[1, P]], channel_multiplier=-1))
            link(pool.memset(lvl_mask[:], 0.0))
            for i, h in enumerate(LEVELS):
                right = lvl_mask[:, i, :].rearrange("p (b two j) -> p b two j", two=2, j=h)[:, :, 1, :]
                nb = P // (2 * h)
                one = ones[:, 0:P // 2].rearrange("p (b j) -> p b j", j=h)
                link(pool.affine_select(out=right, in_=one, compare_op=ALU.is_ge, fill=0.0, base=0,
                                        pattern=[[-2 * h, nb], [0, h]], channel_multiplier=1))
                link(pool.affine_select(out=right, in_=right, compare_op=ALU.is_ge, fill=0.0, base=h - 1,
                                        pattern=[[2 * h, nb], [0, h]], channel_multiplier=-1))
            link(pool.memset(keep[:], 1.0))
            link(pool.memset(keep[:, 0:TP].rearrange("p (a t) -> p a t", t=P)[:, :, 0:1], 0.0))
            link(pool.memset(keep[:, TP:T].rearrange("p (a t) -> p a t", t=DS)[:, :, 0:1], 0.0))
            link(pool.iota(col_iota[:], pattern=[[1, P]], base=0, channel_multiplier=0,
                           allow_small_or_imprecise_dtypes=True))
            link(pool.tensor_copy(rep8[:].rearrange("p (b s) -> p b s", s=DS),
                                  ident[0:DS, 0:DS].unsqueeze(1).to_broadcast([DS, NB, DS])))
            link(pool.affine_select(out=in_seq[:], in_=ones[0:TS, 0:NB], compare_op=ALU.is_ge, fill=0.0, base=0,
                                    pattern=[[-DS, NB]], channel_multiplier=1))
            link(pool.affine_select(out=in_seq[:], in_=in_seq[:], compare_op=ALU.is_ge, fill=0.0, base=DS - 1,
                                    pattern=[[DS, NB]], channel_multiplier=-1))
            link(pool.affine_select(out=same_seq[:].rearrange("p (b s) -> p b s", s=DS),
                                    in_=in_seq[:].unsqueeze(2).to_broadcast([TS, NB, DS]), compare_op=ALU.is_ge,
                                    fill=0.0, base=0, pattern=[[DS, NB], [1, DS]], channel_multiplier=-1))
            link(pool.affine_select(out=lower_e[:], in_=ones[:, 0:NE * NE].rearrange("p (i j) -> p i j", j=NE),
                                    compare_op=ALU.is_ge, fill=0.0, base=-1, pattern=[[1, NE], [-1, NE]],
                                    channel_multiplier=0))
            link(pool.memset(eps[:, 0:1], LN_EPS))
            pool.memset(eps[:, 1:2], RMS_EPS).then_inc(consts.sem, 1)
            for l in range(DEPTH):
                if l == 0:
                    pool.wait_ge(h_ready.sem, 1)
                else:
                    pool.wait_ge(x_ready.sem, x_ready.at(l - 1, 1))
                pool.dma_start(ws[:], a_ws[l].rearrange("h t s -> t h s")).then_inc(prep_in.sem, 16)
                pool.dma_start(bsr[:], a_bs[l:l + 1]).then_inc(prep_in.sem, 16)
                pool.dma_start(lnw, a_ln_w[l].partition_broadcast(P)).then_inc(prep_in.sem, 16)
                pool.dma_start(lnb, a_ln_b[l].partition_broadcast(P)).then_inc(prep_in.sem, 16)
                for h in range(2):
                    pool.dma_start(st[:, h], state_hgrn[l, :, h].rearrange("b d v -> d b v")).then_inc(st_in[h].sem, 16)
                pool.memset(S[:], 0.0).then_inc(consts.sem, 1)
                pool.wait_ge(ws_read.sem, ws_read.at(l, 0))
                pool.affine_select(out=wsT[:], in_=wsT[:], compare_op=ALU.is_ge, fill=0.0, base=0,
                                   pattern=[[0, H], [1, P]], channel_multiplier=-1).then_inc(ws_masked.sem, 1)
                pool.wait_ge(vn_ready.sem, vn_ready.at(l))
                pool.dma_start(chunkv_prompt[l, 0], vtok[:, 1, :]).then_inc(io_out.sem, 16)
                pool.dma_start(chunkv_sample[l].rearrange("b s a -> (b s) a"), vtok[0:TS, 2, :]).then_inc(io_out.sem, 16)
                for h in range(H):
                    pool.wait_ge(st_new.sem, st_new.at(l, h))
                    pool.dma_start(st_sample[l, :, h].rearrange("b d v -> d b v"), st[:, h % 2]).then_inc(st_out[h % 2].sem, 16)
                    if h + 2 < H:
                        pool.wait_ge(st_out[h % 2].sem, 16 * st_out[0].at(l, h // 2))
                        pool.dma_start(st[:, h % 2], state_hgrn[l, :, h + 2].rearrange("b d v -> d b v")).then_inc(st_in[h % 2].sem, 16)
                pool.wait_ge(sp_ready.sem, sp_ready.at(l, 1))
                pool.dma_start(st_prompt[l, 0].rearrange("h d v -> d h v"), stp[:]).then_inc(io_out.sem, 16)


        def loaded(eng, n):
            eng.wait_ge(raw_in[n % RAW].sem, 16 * (n // RAW + 1))

        def chunk_end(key):
            kind, l, c = key
            if kind == "win":
                w = WIN_ORDER.index(c)
                tiles = sum(NT if WIN_ORDER[v] // 2 in (1, 4) else 2 for v in range(w + 1))
                return proj.sem, proj.at(l, tiles - 1)
            if kind == "wout":
                return wo_mm.sem, wo_mm.at(l, 2 * c + 1)
            if kind == "gate":
                return g_mm.sem, g_mm.at(c, 1)
            if kind == "up":
                return u_mm.sem, u_mm.at(c, 1)
            return d_mm.sem, d_mm.at(c, KD - 1)

        def moe_end(j, it):
            kind, c = MOE_ORDER[j]
            s_ = {"gate": eg_mm, "up": eu_mm, "down": ed_mm}[kind]
            return s_.sem, s_.at(it, c)

        def ada_bank(l, c):
            if l:
                return (6, 5)[c % 2]
            return 6 if ADA_A <= c < ADA_A + NWIN else (6, 7)[c % 2]

        split_keys = [key for key in stream if key[0] != "ada"]
        sel, comb, posm = lg[:, 3], lg[:, 5], lg[:, 6]
        TOP_K = 2
        GX_BANKS, SC_BANKS = (0, 4), (7, 2, 0, 4)
        NROWS, NFIRST = 7 * DEPTH + 5, 2 * NT + 1
        VTILES = [(0, 0, P), (1, P, P), (2, TP, TS)]

        @block.tensor
        def _(pe):
            def split_mm(out, xh, xl, wh, wl, start, stop, w_moves=False):
                if w_moves:
                    pe.matmul(out, xh, wh, start=start, stop=False)
                    pe.matmul(out, xh, wl, start=False, stop=False)
                    return pe.matmul(out, xl, wh, start=False, stop=stop)
                pe.matmul(out, wh, xh, start=start, stop=False)
                pe.matmul(out, wh, xl, start=False, stop=False)
                return pe.matmul(out, wl, xh, start=False, stop=stop)

            adas = [0, 0]

            def ada(l, c):
                n = stream.index(("ada", l, c))
                loaded(pe, n)
                if c == 0 and l == 0:
                    pe.wait_ge(first_read.sem, NFIRST)
                before_it = [i for i in range(adas[0]) if ada_bank(*divmod(i, NADA)) == ada_bank(l, c)]
                if before_it:
                    pe.wait_ge(ada_row.sem, before_it[-1] + 1)
                w = slot_as(raw, n % RAW, "ada")
                b = bank[ada_bank(l, c)]
                for kk in range(KD):
                    last = pe.matmul(b[0:NC, 0:CW], cT[:, kk, :], w[:, kk, :], start=(kk == 0), stop=(kk == KD - 1))
                last.then_inc(ada_used.sem, 1)
                adas[0] += 1
                if adas[0] - adas[1] == 2:
                    ada_turn()

            def ada_turn():
                i = adas[1]
                l, c = divmod(i, NADA)
                if c == 0:
                    pe.wait_ge(*((mod_read.sem, mod_read.at(l - 1, 1)) if l else (vec_ready.sem, 1)))
                if c == ADA_A:
                    pe.wait_ge(mod_read.sem, mod_read.at(l, 0))
                pe.wait_ge(ada_row.sem, i + 1)
                for m in range(2):
                    o = (2 * c + m) * NC
                    last = pe.transpose(bank[0][:, o:o + NC], nmean[0:NC, m * P:(m + 1) * P], ident[0:NC, 0:NC])
                last.then_inc(ada_T.sem, 1)
                adas[1] += 1

            def split_chunk(key):
                i = split_index[key]
                pe.wait_ge(lo_ready.sem, i + 1)
                return [slot_as(b, i % SPL, key[0]) for b in (w_hi, w_lo)]

            n_proj = [0]

            def win(l, w):
                wh, wl = split_chunk(("win", l, WIN_ORDER[w]))
                tok = WIN_ORDER[w] // 2 in (1, 4)
                for m in range(NT if tok else 2):
                    if n_proj[0] >= 2:
                        pe.wait_ge(proj_read.sem, n_proj[0] - 1)
                    b = bank[1 + n_proj[0] % 2]
                    for kk in range(KD):
                        if w == 0 and m == 0 and kk % 4 == 0:
                            pe.wait_ge(h_lo.sem, h_lo.at(l, kk // 4))
                        if tok:
                            t0, n = TILES[m]
                            last = split_mm(b[0:n, 0:CW], act_hi[:, kk, t0:t0 + n], act_lo[:, kk, t0:t0 + n],
                                            wh[:, kk, :], wl[:, kk, :], kk == 0, kk == KD - 1, w_moves=True)
                        else:
                            cols = slice(m * P, (m + 1) * P)
                            last = split_mm(b[:, 0:T], act_hi[:, kk, :], act_lo[:, kk, :],
                                            wh[:, kk, cols], wl[:, kk, cols], kk == 0, kk == KD - 1)
                    last.then_inc(proj.sem, 1)
                    n_proj[0] += 1

            def level(l, i):
                if i < NL - 1:
                    pe.wait_ge(Z_ready.sem, Z_ready.at(l, i))
                if i:
                    pe.wait_ge(P_read.sem, P_read.at(l, i - 1))
                a, b = (Z, Z) if i < NL - 1 else (k, q)
                small = i == NL - 1 or LEVELS[i] < DS
                for t, t0, n in VTILES[:3 if small else 2]:
                    for h in range(H):
                        last = pe.matmul(bank[3 + t][0:n, h * P:h * P + n], a[:, h, t0:t0 + n], b[:, h, t0:t0 + n],
                                         start=True, stop=True)
                last.then_inc(lvl_done.sem, 1)

            def layer_norm(l, i):
                pe.wait_ge(z_ready.sem, z_ready.at(l, i))
                for kk in range(KD):
                    last = pe.matmul(bank[7][:, 0:T], ones[:], xT[:, kk, :], start=(kk == 0), stop=(kk == KD - 1))
                last.then_inc(mean_mm.sem, 1)
                for kk in range(KD):
                    if kk % 4 == 0:
                        pe.wait_ge(sq_ready.sem, sq_ready.at(l, 2 * i + kk // 4))
                    last = pe.matmul(bank[6][:, 0:T], ones[:], hf[:, kk, :], start=(kk == 0), stop=(kk == KD - 1))
                last.then_inc(var_mm.sem, 1)

            pe.wait_ge(rows_in.sem, 16 * NROWS)
            pe.wait_ge(consts.sem, 1)
            pe.wait_ge(crow_silu.sem, 1)
            n = 0
            for t, t0, nt in VTILES:
                for half in range(2):
                    if n >= 2:
                        pe.wait_ge(first_read.sem, n - 1)
                    for kk in range(4):
                        f0 = (4 * half + kk) * P
                        last = pe.transpose(bank[1 + n % 2][:, kk * nt:(kk + 1) * nt], xtok[0:nt, t, f0:f0 + P],
                                            ident[0:nt, 0:nt])
                    last.then_inc(first_T.sem, 1)
                    n += 1
            for kk in range(KD):
                last = pe.transpose(bank[3][:, kk * NC:(kk + 1) * NC], crow[:, kk * P:(kk + 1) * P], ident[0:NC, 0:NC])
            last.then_inc(first_T.sem, 1)
            for l in range(DEPTH):
                last = pe.transpose(bank[4][:, l * NV:(l + 1) * NV], vrow[:, l, :], ident[0:NV, 0:NV])
            last.then_inc(first_T.sem, 1)

            for l in range(DEPTH):
                if l == 0:
                    for c in range(ADA_A):
                        ada(0, c)
                    ada_turn()
                for w in range(NWIN):
                    win(l, w)
                    if w == 1:
                        pe.wait_ge(prep_in.sem, 16 * 4 * (l + 1))
                        for h in range(H):
                            last = pe.transpose(bank[7][:, h * P:(h + 1) * P], ws[:, h, :], ident[:])
                        last.then_inc(ws_T.sem, 1)
                    if l == 0:
                        ada(0, ADA_A + w)
                    if w == 3:
                        pe.wait_ge(ws_masked.sem, l + 1)
                        for h in range(H):
                            last = pe.matmul(bank[7][0:TS, h * TS:(h + 1) * TS], rep8[:],
                                             wsT[0:DS, h, 0:DS].unsqueeze(1).to_broadcast([DS, NB, DS]),
                                             start=True, stop=True)
                        last.then_inc(ws_T.sem, 1)
                    if w > NWIN - NL:
                        level(l, w - (NWIN - NL) - 1)
                level(l, NL - 1)
                if l == 0:
                    for c in range(ADA_A + NWIN, NADA):
                        if c == ADA_A + NWIN + 1:
                            pe.wait_ge(ws_read.sem, ws_read.at(0, 1))
                        ada(0, c)
                    ada_turn()
                pe.wait_ge(vn_ready.sem, vn_ready.at(l))
                pe.wait_ge(ws_read.sem, ws_read.at(l, 1))
                for t, t0, n in VTILES:
                    if t == 2:
                        pe.wait_ge(mx_read.sem, mx_read.at(l, 0))
                    b = bank[6 + t % 2]
                    for h in range(H):
                        out = b[:, h * n:(h + 1) * n]
                        if t < 2:
                            pe.matmul(out, vtok[:, t, h * P:(h + 1) * P], wsT[:, h, :], start=True, stop=False)
                            last = pe.matmul(out, ones[0:1, :], bsr[0:1, h, :], start=False, stop=True)
                        else:
                            pe.matmul(out, vtok[0:n, t, h * P:(h + 1) * P], wsS[:, h, :], start=True, stop=False)
                            last = pe.matmul(out, ones[0:1, :], bsr[0:1, h, 0:DS].unsqueeze(1).to_broadcast([1, NB, DS]),
                                             start=False, stop=True)
                    last.then_inc(mx_mm.sem, 1)
                pe.wait_ge(qk_ready.sem, qk_ready.at(l))
                for t, t0, n in VTILES:
                    for h in range(H):
                        last = pe.transpose(bank[3 + t][0:n, h * P:(h + 1) * P], k[:, h, t0:t0 + n], ident[:])
                    last.then_inc(kd_T.sem, 1)
                pe.wait_ge(kd_ready.sem, kd_ready.at(l, 2))
                pe.wait_ge(mx_read.sem, mx_read.at(l, 2))
                for h in range(H):
                    hs = slice(h * P, (h + 1) * P)
                    last = pe.matmul(bank[6][:, hs], kd[:, 0, hs], itok[:, 0, hs], start=True, stop=True)
                last.then_inc(sp_mm.sem, 1)
                pe.wait_ge(proj_read.sem, proj_read.at(l, NEV - 1))
                pe.wait_ge(sp_ready.sem, sp_ready.at(l, 0))
                extra = list(range(NADA)) if l == 0 else []
                for h in range(H):
                    hs = slice(h * P, (h + 1) * P)
                    if h >= 2:
                        pe.wait_ge(o_ready.sem, o_ready.at(l, h - 2))
                    pe.wait_ge(st_in[h % 2].sem, 16 * st_in[0].at(l, h // 2))
                    o = bank[1 + h % 2]
                    pe.matmul(o[:, 0:P], itok[:, 0, hs], S[:, h, 0:P], start=True, stop=True)
                    pe.matmul(o[:, P:TP], itok[:, 1, hs], S[:, h, P:TP], start=True, stop=False)
                    pe.matmul(o[:, P:TP], stp[:, h, :], q[:, h, P:TP], start=False, stop=True)
                    for b in range(NB):
                        tt = slice(TP + b * DS, TP + (b + 1) * DS)
                        pe.matmul(o[:, tt], itok[0:TS, 2, hs], S[0:TS, h, tt], start=True, stop=False)
                        last = pe.matmul(o[:, tt], st[:, h % 2, b, :], q[:, h, tt], start=False, stop=True)
                    last.then_inc(o_mm.sem, 1)
                    pe.wait_ge(ix_ready.sem, ix_ready.at(l, h))
                    if h:
                        pe.wait_ge(st_new.sem, st_new.at(l, h - 1))
                    for half in range(2):
                        last = pe.matmul(bank[3 + half][:, :], kd[0:TS, 2, hs],
                                         iexp[:, 4 * half:4 * half + 4, :].rearrange("s b v -> s (b v)"),
                                         start=True, stop=True)
                    last.then_inc(su_mm.sem, 1)
                    for c in extra[6 * h:6 * h + 6]:
                        ada(1, c)
                    if extra and h == H - 1:
                        ada_turn()
                    pe.wait_ge(o_ready.sem, o_ready.at(l, h))
                    if h:
                        pe.wait_ge(rs_ready.sem, rs_ready.at(l, h - 1))
                    pe.matmul(bank[7][:, 0:T], ones[:], D_[:, h, :], start=True, stop=True).then_inc(ms_mm.sem, 1)
                for h in range(H):
                    hs = slice(h * P, (h + 1) * P)
                    last = pe.matmul(bank[6][:, hs], kd[:, 1, hs], itok[:, 1, hs], start=True, stop=True)
                last.then_inc(sp_mm.sem, 1)
                for c in range(NWO):
                    wh, wl = split_chunk(("wout", l, c))
                    for m in range(2):
                        j = 2 * c + m
                        if j >= 2:
                            pe.wait_ge(wo_read.sem, wo_read.at(l, j - 2))
                        cols = slice(m * P, (m + 1) * P)
                        for kk in range(KD):
                            if j == 0 and kk in (0, KD // 2):
                                pe.wait_ge(mix_lo.sem, mix_lo.at(l, kk // (KD // 2)))
                            last = split_mm(bank[1 + j % 2][:, 0:T], act_hi[:, kk, :], act_lo[:, kk, :],
                                            wh[:, kk, cols], wl[:, kk, cols], kk == 0, kk == KD - 1)
                        last.then_inc(wo_mm.sem, 1)
                layer_norm(l, 0)
                if l == 0:
                    for kind, c in FFN_ORDER:
                        wh, wl = split_chunk((kind, 0, c))
                        if kind == "down":
                            pe.wait_ge(a_lo.sem, a_lo.at(c))
                            for m in range(KD):
                                i = KD * c + m
                                if i >= 3:
                                    pe.wait_ge(d_read.sem, i - 2)
                                for j in range(2):
                                    last = split_mm(bank[5 + i % 3][:, 0:T], dT_hi[:, j, :], dT_lo[:, j, :],
                                                    wh[:, j, m * P:(m + 1) * P], wl[:, j, m * P:(m + 1) * P],
                                                    j == 0, j == 1)
                                last.then_inc(d_mm.sem, 1)
                            continue
                        done, read, b0 = (g_mm, g_read, 1) if kind == "gate" else (u_mm, a_ready, 3)
                        for m in range(2):
                            if c:
                                pe.wait_ge(read.sem, read.at(c - 1, m))
                            for kk in range(KD):
                                if (kind, c, m) == ("gate", 0, 0) and kk % 4 == 0:
                                    pe.wait_ge(h_lo.sem, h_lo.at(l, 2 + kk // 4))
                                last = split_mm(bank[b0 + m][:, 0:T], act_hi[:, kk, :], act_lo[:, kk, :],
                                                wh[:, kk, m * P:(m + 1) * P], wl[:, kk, m * P:(m + 1) * P],
                                                kk == 0, kk == KD - 1)
                            last.then_inc(done.sem, 1)
                    layer_norm(l, 1)

            pe.wait_ge(h_ready.sem, h_ready.at(DEPTH - 1, 3))
            for t, t0, n in VTILES:
                for kk in range(KD):
                    last = pe.matmul(bank[5][0:n, t * NE:(t + 1) * NE], hf[:, kk, t0:t0 + n], w_rt[:, kk, :],
                                     start=(kk == 0), stop=(kk == KD - 1))
            last.then_inc(rt_mm.sem, 1)
            i = 0
            for t, t0, n in VTILES:
                for half in range(2):
                    if i >= 4:
                        pe.wait_ge(h2_lo.sem, i - 3)
                    for kk in range(4):
                        last = pe.transpose(bank[1 + i % 4][0:n, kk * P:(kk + 1) * P], hf[:, 4 * half + kk, t0:t0 + n],
                                            ident[:])
                    last.then_inc(h2_T.sem, 1)
                    i += 1
            pe.wait_ge(sel_ready.sem, 1)
            for t, t0, n in VTILES:
                for u in range(t):
                    pe.matmul(bank[6][0:n, t * NE:(t + 1) * NE], ones[:, 0:n], sel[:, u, :], start=(u == 0), stop=False)
                pe.matmul(bank[6][0:n, t * NE:(t + 1) * NE], before[0:n, 0:n], sel[0:n, t, :], start=(t == 0), stop=True)
            for t, t0, n in VTILES:
                last = pe.matmul(bank[6][:, NT * NE:(NT + 1) * NE], ones[0:n, :], sel[0:n, t, :],
                                 start=(t == 0), stop=(t == NT - 1))
            last.then_inc(pos_mm.sem, 1)

            pe.wait_ge(h2_lo.sem, 2 * NT)
            pe.wait_ge(rounds_ready.sem, 1)
            rounds = pe.value_load(rounds_i[0:1, 0:1], min_val=1, max_val=NT)
            with pe.Fori(0, rounds) as rd:
                pe.wait_ge(G_ready.sem, G_ready.at(rd))
                def turn(it, c):
                    pe.wait_ge(ea_ready.sem, ea_ready.at(it, c))
                    if c:
                        pe.wait_ge(ea_lo.sem, ea_lo.at(it, c - 1))
                    for j in range(2):
                        last = pe.transpose(bank[7][:, j * P:(j + 1) * P],
                                            aa[:, c % 2 * CW + j * P:c % 2 * CW + (j + 1) * P], ident[:])
                    last.then_inc(eT_mm.sem, 1)

                def gather(e):
                    slots = slice(e, e + 1) if isinstance(e, int) else bass.ds(e, 1)
                    for half in range(2):
                        for kk in range(4):
                            f0 = (4 * half + kk) * P
                            out = bank[GX_BANKS[half]][:, kk * P:(kk + 1) * P]
                            for i, part in enumerate((tok_hi, tok_lo)):
                                for t, t0, n in VTILES:
                                    last = pe.matmul(out, part[0:n, t, f0:f0 + P],
                                                     G[0:n, t, slots, :].rearrange("p o s -> p (o s)"),
                                                     start=(i == 0 and t == 0), stop=(i == 1 and t == NT - 1))
                        last.then_inc(gx_mm.sem, 1)

                def chunk(it, j):
                    kind, c = MOE_ORDER[j]
                    pe.wait_ge(lo_ready.sem, it * NMC + (NSPLIT + j + 1))
                    wh, wl = [slot_as(b, (NSPLIT + j) % SPL, kind) for b in (w_hi, w_lo)]
                    if kind == "down":
                        pe.wait_ge(ea_lo.sem, ea_lo.at(it, c))
                        for i in range(2):
                            for half in range(2):
                                cols = slice(512 * half, 512 * half + 512)
                                last = split_mm(bank[5 + half][:, :], aT_hi[:, i, :], aT_lo[:, i, :],
                                                wh[:, i, cols], wl[:, i, cols], c == 0 and i == 0,
                                                c == NFC - 1 and i == 1, w_moves=True)
                        last.then_inc(ed_mm.sem, 1)
                        return
                    done, read, b0 = (eg_mm, eg_read, 1) if kind == "gate" else (eu_mm, ea_ready, 3)
                    if j == 0:
                        pe.wait_ge(xg_lo_ready.sem, xg_lo_ready.at(it, 1))
                    if (kind, c) == ("gate", 1):
                        pe.wait_ge(sc_read.sem, it * KD + 1)
                    if c >= 2:
                        pe.wait_ge(read.sem, read.at(it, c - 2))
                    for kk in range(KD):
                        last = split_mm(bank[b0 + c % 2][:, 0:CW], xg_hi[:, kk, :], xg_lo[:, kk, :],
                                        wh[:, kk, :], wl[:, kk, :], kk == 0, kk == KD - 1, w_moves=True)
                    last.then_inc(done.sem, 1)

                def rest_of(it, following):
                    for j in range(1, NMC):
                        kind, c = MOE_ORDER[j]
                        if kind == "up" and c:
                            turn(it, c - 1)
                        if j == NMC - 1:
                            turn(it, c)
                            if following is not None:
                                gather(following)
                        chunk(it, j)

                def scatter(it, e):
                    slots = slice(e, e + 1) if isinstance(e, int) else bass.ds(e, 1)
                    to_tok = GT[:, slots, :].rearrange("p o t -> p (o t)")
                    for m in range(KD):
                        pe.wait_ge(yw_lo.sem, yw_lo.at(it, m // 4))
                        if m >= 4:
                            pe.wait_ge(sc_read.sem, sc_read.at(it, m - 4))
                        out = bank[SC_BANKS[m % 4]][:, 0:T]
                        pe.matmul(out, y_hi[:, m * P:(m + 1) * P], to_tok, start=True, stop=False)
                        pe.matmul(out, y_lo[:, m * P:(m + 1) * P], to_tok, start=False, stop=True).then_inc(sc_mm.sem, 1)

                first = pe.snap(rd * NE)
                gather(0)
                for e in range(NE):
                    if e >= 2:
                        pe.wait_ge(GT_read.sem, GT_read.at(rd, e - 2))
                    for t, t0, n in VTILES:
                        last = pe.transpose(bank[2 + e % 2][:, t0:t0 + n], G[0:n, t, e, :].bitcast(F32), ident[0:n, 0:n])
                    last.then_inc(GT_mm.sem, 1)
                for e in range(NE):
                    for t, t0, n in VTILES:
                        last = pe.matmul(bank[5][:, e:e + 1], G[0:n, t, e, :].bitcast(F32), comb[0:n, t, e:e + 1],
                                         start=(t == 0), stop=(t == NT - 1))
                last.then_inc(wsl_mm.sem, 1)
                pe.wait_ge(GT_read.sem, GT_read.at(rd, NE - 1))
                chunk(first, 0)
                with pe.Fori(0, NE - 1) as e:
                    it = pe.snap(rd * NE + e)
                    following = pe.snap(rd * NE + e + 1)
                    rest_of(it, pe.snap(e + 1))
                    chunk(following, 0)
                    scatter(it, e)
                it = pe.snap(rd * NE + (NE - 1))
                rest_of(it, None)
                scatter(it, NE - 1)
            layer_norm(DEPTH - 1, 1)
            pe.wait_ge(x_ready.sem, x_ready.at(DEPTH - 1, 1))
            i = 0
            for t, t0, n in VTILES:
                for half in range(2):
                    if i >= 4:
                        pe.wait_ge(out_read.sem, i - 3)
                    for kk in range(4):
                        last = pe.transpose(bank[1 + i % 4][0:n, kk * P:(kk + 1) * P], xT[:, 4 * half + kk, t0:t0 + n],
                                            ident[:])
                    last.then_inc(out_T.sem, 1)
                    i += 1

        @block.scalar
        def _(act):
            links = [0]

            def link(ins):
                links[0] += 1
                ins.then_inc(act_link.sem, 1)
                act.wait_ge(act_link.sem, links[0])

            done = [0]

            def make_hi(upto):
                while done[0] <= min(upto, NSPLIT - 1):
                    i = done[0]
                    loaded(act, stream.index(split_keys[i]))
                    if i >= SPL:
                        act.wait_ge(*chunk_end(split_keys[i - SPL]))
                    act.activation(w_hi[:, i % SPL, :], raw[:, place[split_keys[i]], :], ACT.Copy).then_inc(hi_ready.sem, 1)
                    done[0] += 1

            def ada_rows(l, c):
                i = ada_index[("ada", l, c)]
                act.wait_ge(ada_used.sem, i + 1)
                if i:
                    act.wait_ge(ada_T.sem, i)
                act.activation(nmean[0:NC, 0:CW], bank[ada_bank(l, c)][0:NC, 0:CW], ACT.Copy).then_inc(ada_row.sem, 1)

            def halves(src, ready, ready_at, sig, sig_l, dst):
                for a in range(2):
                    act.wait_ge(ready.sem, ready_at(a))
                    act.activation(dst[:, 4 * a:4 * a + 4, :], src[:, 4 * a:4 * a + 4, :], ACT.Copy).then_inc(sig.sem, 1)

            def layer_norm(l, i):
                act.wait_ge(mean_mm.sem, mean_mm.at(l, i))
                act.activation(nmean[:], bank[7][:, 0:T], ACT.Copy, scale=-1.0 / D).then_inc(mean_ready.sem, 1)
                if i == 0:
                    act.wait_ge(io_out.sem, 48 * (l + 1))
                    for s_ in st_out:
                        act.wait_ge(s_.sem, 16 * s_.at(l, H // 2 - 1))
                for a in range(2):
                    act.wait_ge(zc_ready.sem, zc_ready.at(l, 2 * i + a))
                    act.activation(hf[:, 4 * a:4 * a + 4, :], xT[:, 4 * a:4 * a + 4, :], ACT.Square).then_inc(sq_ready.sem, 1)
                act.wait_ge(var_mm.sem, var_mm.at(l, i))
                act.activation(nmean[:], bank[6][:, 0:T], ACT.Sqrt, scale=1.0 / D, bias=eps[:, 0:1]).then_inc(sd_ready.sem, 1)

            act.wait_ge(rows_in.sem, 16 * NROWS)
            act.activation(crow[:], crow[:], ACT.Silu).then_inc(crow_silu.sem, 1)
            act.wait_ge(vec_ready.sem, 1)
            act.activation(lt[:, 2:4, :], lt[:, 0:2, :], ACT.Exp).then_inc(lt_exp.sem, 1)
            evs = [0]
            for c in range(ADA_A):
                ada_rows(0, c)
            for l in range(DEPTH):
                halves(hmix, h_ready, lambda a: h_ready.at(l, a), h_hi, l, act_hi)
                base = split_index[("win", l, WIN_ORDER[0])]
                for w in range(NWIN):
                    make_hi(min(base + w + 2, base + NWIN - 1))
                    what, half = WIN_ORDER[w] // 2, WIN_ORDER[w] % 2
                    for m in range(NT if what in (1, 4) else 2):
                        act.wait_ge(proj.sem, evs[0] + 1)
                        b = bank[1 + evs[0] % 2]
                        evs[0] += 1
                        if what in (1, 4):
                            t0, n = TILES[m]
                            dst = (vtok if what == 1 else itok)[0:n, m, half * CW:(half + 1) * CW]
                            src, func = b[0:n, 0:CW], ACT.Gelu if what == 1 else ACT.Copy
                        else:
                            t = 2 * half + m
                            dst = {0: ug[:, t, :], 2: q[:, t, :], 3: fe[:, t, :], 5: ug[:, H + t, :]}[what]
                            src = b[:, 0:T]
                            func = {0: ACT.Gelu, 2: ACT.Silu, 3: ACT.Sigmoid, 5: ACT.Silu}[what]
                        act.activation(dst, src, func).then_inc(proj_read.sem, 1)
                    if w == 1:
                        act.wait_ge(ws_T.sem, ws_T.at(l, 0))
                        act.activation(wsT[:].rearrange("p h t -> p (h t)"), bank[7][:, :], ACT.Copy).then_inc(ws_read.sem, 1)
                    if w == 2:
                        act.wait_ge(fg_ready.sem, fg_ready.at(l))
                        act.activation(fe[:], fe[:], ACT.Ln).then_inc(lf_ready.sem, 1)
                    if w == 3:
                        act.wait_ge(bc_ready.sem, bc_ready.at(l))
                        act.activation(fe[:], bc[:], ACT.Exp).then_inc(eb_ready.sem, 1)
                    if w >= 4 and w - 4 < NL - 1:
                        i = w - 4
                        n = T if LEVELS[i] < DS else TP
                        act.wait_ge(D_ready.sem, D_ready.at(l, i))
                        act.activation(D_[:, :, 0:n], D_[:, :, 0:n], ACT.Exp).then_inc(E_ready.sem, 1)
                    if w == 8:
                        act.wait_ge(v_var.sem, v_var.at(l))
                        act.activation(vmv[:, :, 2], vmv[:, :, 1], ACT.Sqrt, bias=eps[:, 0:1]).then_inc(v_sd.sem, 1)
                    if l == 0:
                        ada_rows(0, ADA_A + w)
                if l == 0:
                    for c in range(ADA_A + NWIN, NADA):
                        ada_rows(0, c)
                act.wait_ge(D_ready.sem, D_ready.at(l, NL - 1))
                act.activation(D_[:], D_[:], ACT.Exp).then_inc(E_ready.sem, 1)
                for t, t0, n in VTILES:
                    act.wait_ge(kd_T.sem, kd_T.at(l, t))
                    act.activation(kd[0:n, t, :], bank[3 + t][0:n, :], ACT.Copy).then_inc(kd_ready.sem, 1)
                act.wait_ge(sp_mm.sem, sp_mm.at(l, 0))
                act.activation(stp[:].rearrange("p h v -> p (h v)"), bank[6][:, :], ACT.Copy).then_inc(sp_ready.sem, 1)
                act.wait_ge(mx_read.sem, mx_read.at(l, 2))
                act.activation(act_hi[:, 0:H, :], ug[:, 0:H, :], ACT.Copy).then_inc(mix_hi.sem, 1)
                for h in range(H):
                    act.wait_ge(o_mm.sem, o_mm.at(l, h))
                    act.activation(Z[:, h, :], bank[1 + h % 2][:, 0:T], ACT.Copy)
                    act.activation(D_[:, h, :], bank[1 + h % 2][:, 0:T], ACT.Square).then_inc(o_ready.sem, 1)
                    if l == 0:
                        for c in range(6 * h, 6 * h + 6):
                            ada_rows(1, c)
                    act.wait_ge(ms_mm.sem, ms_mm.at(l, h))
                    link(act.activation(D_[:, h, :], bank[7][:, 0:T], ACT.Ln, scale=1.0 / P, bias=eps[:, 1:2]))
                    act.activation(D_[:, h, :], D_[:, h, :], ACT.Exp, scale=-0.5).then_inc(rs_ready.sem, 1)
                base = split_index[("wout", l, 0)]
                make_hi(base + 1)
                act.wait_ge(b_ready.sem, b_ready.at(l))
                act.activation(act_hi[:, H:2 * H, :], ug[:, H:2 * H, :], ACT.Copy).then_inc(mix_hi.sem, 1)
                base = split_index[("wout", l, 0)]
                make_hi(base + NWO - 1 + (SPL if l == 0 else 0))
                layer_norm(l, 0)
                halves(hf, h_ready, lambda a: h_ready.at(l, 2 + a), h_hi, l, act_hi)
                if l == 0:
                    at = {key: split_index[(key[0], 0, key[1])] for key in FFN_ORDER}
                    for c in range(NFC):
                        make_hi(at[("gate", c)] + 2)
                        for m in range(2):
                            act.wait_ge(g_mm.sem, g_mm.at(c, m))
                            if c:
                                act.wait_ge(a_ready.sem, a_ready.at(c - 1, m))
                            act.activation(sil[:, m * T:(m + 1) * T], bank[1 + m][:, 0:T], ACT.Silu).then_inc(g_read.sem, 1)
                        make_hi(at[("up", c)] + 2)
                        act.wait_ge(a_ready.sem, a_ready.at(c, 1))
                        if c:
                            act.wait_ge(d_mm.sem, d_mm.at(c - 1, KD - 1))
                        act.activation(dT_hi.rearrange("p j t -> p (j t)"), aa[:, :], ACT.Copy).then_inc(a_hi.sem, 1)
                    make_hi(at[("down", NFC - 1)] + 2)
                    layer_norm(l, 1)

            act.wait_ge(rt_sub.sem, 1)
            act.activation(lg[:, 1], lg[:, 1], ACT.Exp).then_inc(rt_exp.sem, 1)
            for i, (t, half) in enumerate((t, half) for t in range(NT) for half in range(2)):
                n = TILES[t][1]
                act.wait_ge(h2_T.sem, i + 1)
                act.activation(tok_hi[0:n, t, 512 * half:512 * half + 512], bank[1 + i % 4][0:n, :], ACT.Copy).then_inc(h2_hi.sem, 1)
            act.wait_ge(rounds_ready.sem, 1)
            rounds = act.value_load(rounds_i[0:1, 0:1], min_val=1, max_val=NT)
            at_e = {key: j for j, key in enumerate(MOE_ORDER)}
            with act.Fori(0, rounds) as rd:
                def expert_hi(it, first, upto, before=None):
                    for j in range(first, upto + 1):
                        s, use, per = moe_raw(j)
                        act.wait_ge(raw_in[s].sem, it * (16 * per) + 16 * (RAW_USES[s] + use + 1))
                        if j >= SPL:
                            act.wait_ge(*moe_end(j - SPL, it))
                        elif before is not None:
                            act.wait_ge(*moe_end(NMC + j - SPL, before))
                        act.activation(w_hi[:, (NSPLIT + j) % SPL, :], raw[:, s, :], ACT.Copy).then_inc(hi_ready.sem, 1)

                def tokens(it):
                    for half in range(2):
                        act.wait_ge(gx_mm.sem, gx_mm.at(it, half))
                        act.activation(xg_hi[:, 4 * half:4 * half + 4, :].rearrange("p k s -> p (k s)"),
                                       bank[GX_BANKS[half]][:, :], ACT.Copy).then_inc(xg_hi_ready.sem, 1)

                def silu(it, c):
                    act.wait_ge(eg_mm.sem, eg_mm.at(it, c))
                    if c >= 2:
                        act.wait_ge(ea_ready.sem, ea_ready.at(it, c - 2))
                    act.activation(sil[:, c % 2 * CW:(c % 2 + 1) * CW], bank[1 + c % 2][:, 0:CW], ACT.Silu).then_inc(eg_read.sem, 1)

                def turned(it, c):
                    act.wait_ge(eT_mm.sem, eT_mm.at(it, c))
                    if c:
                        act.wait_ge(ed_mm.sem, ed_mm.at(it, c - 1))
                    act.activation(aT_hi.rearrange("p j s -> p (j s)"), bank[7][:, 0:CW], ACT.Copy).then_inc(ea_hi.sem, 1)

                def expert(it, following):
                    silu(it, 0)
                    done_e = SPL
                    for c in range(NFC - 1):
                        upto = min(at_e[("gate", c + 1)] + 2, NMC - 1)
                        expert_hi(it, done_e, upto)
                        done_e = upto + 1
                        silu(it, c + 1)
                        if c == NFC - 2:
                            expert_hi(it, done_e, NMC - 1)
                        turned(it, c)
                    if following is not None:
                        expert_hi(following, 0, 0, before=it)
                    turned(it, NFC - 1)
                    if following is not None:
                        expert_hi(following, 1, 1, before=it)
                        tokens(following)
                    for half in range(2):
                        act.wait_ge(y_read.sem, y_read.at(it, half))
                        act.activation(y_hi[:, 512 * half:512 * half + 512], yf[:, 512 * half:512 * half + 512],
                                       ACT.Copy).then_inc(yw_hi.sem, 1)
                    if following is not None:
                        expert_hi(following, 2, 2, before=it)

                first = act.snap(rd * NE)
                act.wait_ge(sc_read.sem, first * KD + 1)
                expert_hi(first, 0, 0)
                tokens(first)
                for e in range(NE):
                    act.wait_ge(GT_mm.sem, GT_mm.at(rd, e))
                    act.activation(GT[:, e, :], bank[2 + e % 2][:, 0:T], ACT.Copy).then_inc(GT_read.sem, 1)
                expert_hi(first, 1, SPL - 1)
                with act.Fori(0, NE - 1) as e:
                    it = act.snap(rd * NE + e)
                    expert(it, act.snap(rd * NE + e + 1))
                expert(act.snap(rd * NE + (NE - 1)), None)
            layer_norm(DEPTH - 1, 1)
            for i, (t, half) in enumerate((t, half) for t in range(NT) for half in range(2)):
                n = TILES[t][1]
                act.wait_ge(out_T.sem, i + 1)
                act.activation(xtok[0:n, t, 512 * half:512 * half + 512], bank[1 + i % 4][0:n, :], ACT.Copy).then_inc(out_read.sem, 1)

        @block.vector
        def _(dve):
            links = [0]

            def link(ins):
                links[0] += 1
                ins.then_inc(dve_link.sem, 1)
                dve.wait_ge(dve_link.sem, links[0])

            done = [0]

            def make_lo(upto):
                while done[0] <= min(upto, NSPLIT - 1):
                    i = done[0]
                    dve.wait_ge(hi_ready.sem, i + 1)
                    dve.tensor_tensor(w_lo[:, i % SPL, :], raw[:, place[split_keys[i]], :],
                                      w_hi[:, i % SPL, :].bitcast(F32), ALU.subtract).then_inc(lo_ready.sem, 1)
                    done[0] += 1

            def per_seq(m0, n=KD):
                return modT[:, m0:m0 + n, 1:NC].unsqueeze(3).to_broadcast([P, n, NB, DS])

            def samples(ap):
                return ap.rearrange("p k (b s) -> p k b s", s=DS)

            def modulate(l, i, out):
                sh, sc = 3 * KD * i, 3 * KD * i + KD
                for a in range(2):
                    ks = slice(4 * a, 4 * a + 4)
                    link(dve.tensor_tensor(samples(out[:, ks, TP:T]), samples(xT[:, ks, TP:T]), per_seq(sc + 4 * a, 4), ALU.mult))
                    dve.tensor_tensor(samples(out[:, ks, TP:T]), samples(out[:, ks, TP:T]), per_seq(sh + 4 * a, 4), ALU.add)
                    for kk in range(4 * a, 4 * a + 4):
                        last = dve.tensor_scalar(out[:, kk, 0:TP], xT[:, kk, 0:TP], modT[:, sc + kk, 0:1],
                                                 modT[:, sh + kk, 0:1], ALU.mult, ALU.add)
                    last.then_inc(h_ready.sem, 1)
                for a in range(2):
                    ks = slice(4 * a, 4 * a + 4)
                    dve.wait_ge(h_hi.sem, h_hi.at(l, 2 * i + a))
                    dve.tensor_tensor(act_lo[:, ks, :], out[:, ks, :], act_hi[:, ks, :].bitcast(F32),
                                      ALU.subtract).then_inc(h_lo.sem, 1)
                link(dve.tensor_scalar(xT[:], xT[:], ALPHA, None, ALU.mult))

            def layer_norm(l, i, ahead=None):
                nm = nmean[:].unsqueeze(1).to_broadcast([P, KD, T])
                dve.wait_ge(mean_ready.sem, mean_ready.at(l, i))
                for a in range(2):
                    ks = slice(4 * a, 4 * a + 4)
                    dve.tensor_tensor(xT[:, ks, :], xT[:, ks, :], nmean[:].unsqueeze(1).to_broadcast([P, 4, T]),
                                      ALU.add).then_inc(zc_ready.sem, 1)
                if ahead is not None:
                    make_lo(ahead)
                dve.wait_ge(sd_ready.sem, sd_ready.at(l, i))
                link(dve.reciprocal(nmean[:], nmean[:]))
                link(dve.tensor_tensor(xT[:], xT[:], nm, ALU.mult))
                w0 = V_LN2W if i else V_LN1W
                for kk in range(KD):
                    last = dve.tensor_scalar(xT[:, kk, :], xT[:, kk, :], vecT[:, l, w0 + kk:w0 + kk + 1],
                                             vecT[:, l, w0 + KD + kk:w0 + KD + kk + 1], ALU.mult, ALU.add)
                last.then_inc(x_ready.sem, 1)
                dve.wait_ge(x_ready.sem, x_ready.at(l, i))

            def modulation(l, part):
                a, b = (0, 2 * KD) if part == 0 else (2 * KD, NM)
                dve.wait_ge(ada_T.sem, ada_index[("ada", l, (b * P) // CW - 1)] + 1)
                bias = vecT[:, l, V_ADA + a:V_ADA + b].unsqueeze(2).to_broadcast([P, b - a, NC])
                link(dve.tensor_tensor(modT[:, a:b, :], bank[0][:, a * NC:b * NC].rearrange("p (m c) -> p m c", c=NC), bias, ALU.add))
                sc = 4 * KD if part else KD
                ins = dve.tensor_scalar(modT[:, sc:sc + KD, :], modT[:, sc:sc + KD, :], 1.0, None, ALU.add)
                ins.then_inc(mod_read.sem, 1)
                dve.wait_ge(mod_read.sem, mod_read.at(l, part))

            def add_channels(l):
                for m in range(KD):
                    dve.scalar_tensor_tensor(xT[:, m, 0:TP], accT[:, m, 0:TP], modT[:, 5 * KD + m, 0:1], xT[:, m, 0:TP],
                                             ALU.mult, ALU.add)
                link(dve.tensor_tensor(samples(hf[:, :, TP:T]), samples(accT[:, :, TP:T]), per_seq(5 * KD), ALU.mult))
                dve.tensor_tensor(xT[:, :, TP:T], xT[:, :, TP:T], hf[:, :, TP:T], ALU.add).then_inc(z_ready.sem, 1)
                dve.wait_ge(z_ready.sem, z_ready.at(l, 1))

            for i, (t, half) in enumerate((t, half) for t in range(NT) for half in range(2)):
                t0, n = TILES[t]
                dve.wait_ge(first_T.sem, i + 1)
                dve.tensor_copy(xT[:, 4 * half:4 * half + 4, t0:t0 + n],
                                bank[1 + i % 2][:, 0:4 * n].rearrange("p (k t) -> p k t", t=n)).then_inc(first_read.sem, 1)
            dve.wait_ge(first_T.sem, 2 * NT + 1)
            dve.tensor_copy(cT[:], bank[3][:, 0:KD * NC].rearrange("p (k c) -> p k c", c=NC)).then_inc(first_read.sem, 1)
            dve.wait_ge(first_T.sem, 2 * NT + 2)
            link(dve.tensor_copy(vecT[:], bank[4][:, 0:DEPTH * NV].rearrange("p (l v) -> p l v", v=NV)))
            l0, l1 = vecT[:, 0, V_LB:V_LB + H], vecT[:, 1, V_LB:V_LB + H]
            link(dve.tensor_tensor(lt[:, 4, :], l0, l1, ALU.max))
            link(dve.tensor_tensor(lt[:, 0, :], l0, lt[:, 4, :], ALU.subtract))
            link(dve.tensor_tensor(lt[:, 1, :], l1, lt[:, 4, :], ALU.subtract))
            lt_in = dve.tensor_copy(lt[:, 6, :], l0)
            lt_in.then_inc(vec_ready.sem, 1)
            dve.wait_ge(lt_exp.sem, 1)
            link(dve.tensor_tensor(lt[:, 5, :], lt[:, 2, :], lt[:, 3, :], ALU.add))
            link(dve.reciprocal(lt[:, 5, :], lt[:, 5, :]))
            link(dve.tensor_tensor(lt[:, 2:4, :], lt[:, 2:4, :], lt[:, 5:6, :].to_broadcast([P, 2, H]), ALU.mult))
            link(dve.tensor_tensor(lt[:, 3, :], lt[:, 2, :], lt[:, 3, :], ALU.add))
            link(dve.tensor_tensor(lbv[:, 1, 0, :], lt[:, 3, :], lt[:, 2, :], ALU.subtract))
            link(dve.tensor_tensor(lbv[:, 0, 0, :], lt[:, 2, :], lt[:, 2, :], ALU.subtract))
            link(dve.tensor_scalar(lbv[:, :, 1, :], lbv[:, :, 0, :], -1.0, 1.0, ALU.mult, ALU.add))
            for l in range(DEPTH):
                if l == 0:
                    modulation(0, 0)
                modulate(l, 0, hmix)
                base = split_index[("win", l, WIN_ORDER[0])]
                def take(i):
                    dve.wait_ge(lvl_done.sem, lvl_done.at(l, i))
                    if i:
                        dve.wait_ge(P_read.sem, P_read.at(l, i - 1))
                    small = i == NL - 1 or LEVELS[i] < DS
                    for t, t0, n in VTILES[:3 if small else 2]:
                        mask = (ident[0:n, 0:n] if i == NL - 1 else lvl_mask[0:n, i, 0:n]).bitcast(I32)
                        last = dve.copy_predicated(S[0:n, :, t0:t0 + n], mask.unsqueeze(1).to_broadcast([n, H, n]),
                                                   bank[3 + t][0:n, :].rearrange("p (h t) -> p h t", h=H)[:, :, 0:n])
                    last.then_inc(P_read.sem, 1)

                for w in range(NWIN):
                    make_lo(min(base + w + 2, base + NWIN - 1))
                    if w == 2:
                        dve.wait_ge(proj_read.sem, proj_read.at(l, 3))
                        for h in range(H):
                            last = dve.tensor_scalar(fe[:, h, :], fe[:, h, :], lbv[:, l, 1, h:h + 1], lbv[:, l, 0, h:h + 1],
                                                     ALU.mult, ALU.add)
                        link(last)
                        dve.tensor_scalar(k[:], fe[:], -1.0, 1.0, ALU.mult, ALU.add).then_inc(fg_ready.sem, 1)
                    if w == 3:
                        dve.wait_ge(lf_ready.sem, lf_ready.at(l))
                        dve.wait_ge(consts.sem, 2 + l)
                        for h in range(H):
                            last = dve.tensor_tensor_scan(bc[:, h, :], keep[:], fe[:, h, :], 0.0, ALU.mult, ALU.add)
                        last.then_inc(bc_ready.sem, 1)
                        dve.wait_ge(bc_ready.sem, bc_ready.at(l))
                    if w >= 6:
                        take(w - 6)
                    if w == 4:
                        dve.wait_ge(ws_T.sem, ws_T.at(l, 1))
                        dve.tensor_tensor(wsS[:], bank[7][0:TS, 0:H * TS].rearrange("p (h t) -> p h t", h=H),
                                          same_seq[:].unsqueeze(1).to_broadcast([TS, H, TS]), ALU.mult).then_inc(ws_read.sem, 1)

                    def blocks(ap, n, hb):
                        return ap[:, :, 0:n].rearrange("p h (b j) -> p h b j", j=2 * hb)

                    if w >= 4 and w - 4 < NL - 1:
                        i = w - 4
                        hb = LEVELS[i]
                        n = T if hb < DS else TP
                        if i:
                            dve.wait_ge(Z_ready.sem, Z_ready.at(l, i - 1))
                        b4, d4 = blocks(bc, n, hb), blocks(D_, n, hb)
                        mid = b4[:, :, :, hb - 1:hb].to_broadcast([P, H, n // (2 * hb), hb])
                        dve.tensor_tensor(d4[:, :, :, 0:hb], mid, b4[:, :, :, 0:hb], ALU.subtract)
                        dve.tensor_tensor(d4[:, :, :, hb:2 * hb], b4[:, :, :, hb:2 * hb], mid, ALU.subtract).then_inc(D_ready.sem, 1)
                        dve.wait_ge(E_ready.sem, E_ready.at(l, i))
                        if i:
                            dve.wait_ge(lvl_done.sem, lvl_done.at(l, i - 1))
                        dve.wait_ge(proj_read.sem, proj_read.at(l, 7))
                        e4, z4 = blocks(D_, n, hb), blocks(Z, n, hb)
                        dve.tensor_tensor(z4[:, :, :, 0:hb], e4[:, :, :, 0:hb], blocks(k, n, hb)[:, :, :, 0:hb], ALU.mult)
                        dve.tensor_tensor(z4[:, :, :, hb:2 * hb], e4[:, :, :, hb:2 * hb], blocks(q, n, hb)[:, :, :, hb:2 * hb],
                                          ALU.mult).then_inc(Z_ready.sem, 1)

                    if w == 8:
                        dve.wait_ge(proj_read.sem, proj_read.at(l, 8 + 2 * NT + 2 * NT - 1))
                        link(dve.memset(vmv[:], 1.0))
                        for t, t0, n in VTILES:
                            last = dve.bn_stats(vstat[0:n, t, :], vtok[0:n, t, :])
                        link(last)
                        for t, t0, n in VTILES:
                            last = dve.bn_aggr(vmv[0:n, t, 0:2], vstat[0:n, t, :])
                        last.then_inc(v_var.sem, 1)
                        dve.wait_ge(v_sd.sem, v_sd.at(l))
                        link(dve.reciprocal(vmv[:, :, 3], vmv[:, :, 2]))
                    if w in (9, 10, 11):
                        t, t0, n = VTILES[w - 9]
                        link(dve.tensor_scalar(vtok[0:n, t, :], vtok[0:n, t, :], vmv[0:n, t, 0:1], vmv[0:n, t, 3:4],
                                               ALU.subtract, ALU.mult))
                        link(dve.tensor_tensor(vtok[0:n, t, :], vtok[0:n, t, :], lnw[0:n, :], ALU.mult))
                        last = dve.tensor_tensor(vtok[0:n, t, :], vtok[0:n, t, :], lnb[0:n, :], ALU.add)
                        if w == 11:
                            last.then_inc(vn_ready.sem, 1)
                take(NL - 2)
                take(NL - 1)
                dve.wait_ge(P_read.sem, P_read.at(l, NL - 1))
                for h in range(H):
                    for s0, s1, j in ((0, TP, P), (TP, T, DS)):
                        B4 = bc[:, h, s0:s1].rearrange("p (b j) -> p b j", j=j)
                        last = dve.tensor_tensor(D_[:, h, s0:s1].rearrange("p (b j) -> p b j", j=j),
                                                 B4[:, :, j - 1:j].to_broadcast([P, (s1 - s0) // j, j]), B4, ALU.subtract)
                last.then_inc(D_ready.sem, 1)
                dve.wait_ge(eb_ready.sem, eb_ready.at(l))
                dve.tensor_tensor(q[:], q[:], fe[:], ALU.mult)
                dve.wait_ge(E_ready.sem, E_ready.at(l, NL - 1))
                dve.tensor_tensor(k[:], k[:], D_[:], ALU.mult).then_inc(qk_ready.sem, 1)
                for t, t0, n in VTILES:
                    dve.wait_ge(mx_mm.sem, mx_mm.at(l, t))
                    dve.tensor_tensor(ug[:, 0:H, t0:t0 + n], ug[:, 0:H, t0:t0 + n],
                                      bank[6 + t % 2][:, 0:H * n].rearrange("p (h t) -> p h t", h=H), ALU.mult).then_inc(mx_read.sem, 1)
                if l == 0:
                    modulation(0, 1)
                for h in range(H):
                    hs = slice(h * P, (h + 1) * P)
                    if h:
                        dve.wait_ge(su_mm.sem, su_mm.at(l, h - 1))
                    dve.tensor_tensor(iexp, itok[0:TS, 2, hs].unsqueeze(1).to_broadcast([TS, NB, P]),
                                      in_seq[:].unsqueeze(2).to_broadcast([TS, NB, P]), ALU.mult).then_inc(ix_ready.sem, 1)
                    if h == 0:
                        dve.wait_ge(mix_hi.sem, mix_hi.at(l, 0))
                        dve.tensor_tensor(act_lo[:, 0:H, :], ug[:, 0:H, :], act_hi[:, 0:H, :].bitcast(F32),
                                          ALU.subtract).then_inc(mix_lo.sem, 1)
                    dve.wait_ge(su_mm.sem, su_mm.at(l, h))
                    dk = fe[:, h, TP:T].rearrange("p (b j) -> p b j", j=DS)[:, :, DS - 1:DS].to_broadcast([P, NB, P])
                    dve.wait_ge(o_mm.sem, o_mm.at(l, h))
                    link(dve.tensor_tensor(st[:, h % 2], st[:, h % 2], dk, ALU.mult))
                    for half in range(2):
                        bs = slice(4 * half, 4 * half + 4)
                        last = dve.tensor_tensor(st[:, h % 2, bs, :], st[:, h % 2, bs, :],
                                                 bank[3 + half][:, :].rearrange("p (b v) -> p b v", v=P), ALU.add)
                    last.then_inc(st_new.sem, 1)
                    if l == 0 and h == 1:
                        modulation(1, 0)
                    dve.wait_ge(rs_ready.sem, rs_ready.at(l, h))
                    link(dve.tensor_tensor(Z[:, h, :], Z[:, h, :], D_[:, h, :], ALU.mult))
                    last = dve.scalar_tensor_tensor(ug[:, H + h, :], Z[:, h, :], vecT[:, l, V_BN:V_BN + 1], ug[:, H + h, :],
                                                    ALU.mult, ALU.mult)
                    if h == H - 1:
                        last.then_inc(b_ready.sem, 1)
                make_lo(split_index[("wout", l, 0)])
                dve.wait_ge(mix_hi.sem, mix_hi.at(l, 1))
                dve.tensor_tensor(act_lo[:, H:2 * H, :], ug[:, H:2 * H, :], act_hi[:, H:2 * H, :].bitcast(F32),
                                  ALU.subtract).then_inc(mix_lo.sem, 1)
                dve.wait_ge(sp_mm.sem, sp_mm.at(l, 1))
                for h in range(H):
                    last = dve.scalar_tensor_tensor(stp[:, h, :], stp[:, h, :], fe[:, h, TP - 1:TP], bank[6][:, h * P:(h + 1) * P],
                                                    ALU.mult, ALU.add)
                last.then_inc(sp_ready.sem, 1)
                base = split_index[("wout", l, 0)]
                gt = 2 * KD
                for m in range(KD):
                    make_lo(min(base + m // 2 + 2, base + NWO - 1))
                    dve.wait_ge(wo_mm.sem, wo_mm.at(l, m))
                    b = bank[1 + m % 2]
                    dve.scalar_tensor_tensor(xT[:, m, 0:TP], b[:, 0:TP], modT[:, gt + m, 0:1], xT[:, m, 0:TP], ALU.mult, ALU.add)
                    tmp = nmean[:, 0:TS]
                    dve.tensor_tensor(tmp.rearrange("p (b s) -> p b s", s=DS), b[:, TP:T].rearrange("p (b s) -> p b s", s=DS),
                                      modT[:, gt + m, 1:NC].unsqueeze(2).to_broadcast([P, NB, DS]), ALU.mult).then_inc(wo_read.sem, 1)
                    dve.wait_ge(wo_read.sem, wo_read.at(l, m))
                    last = dve.tensor_tensor(xT[:, m, TP:T], xT[:, m, TP:T], tmp, ALU.add)
                    if m < KD - 1:
                        link(last)
                last.then_inc(z_ready.sem, 1)
                if l == 0:
                    make_lo(base + NWO + 1)
                layer_norm(l, 0, base + NWO + 2 if l == 0 else None)
                modulate(l, 1, hf)
                if l == 0:
                    at = {key: split_index[(key[0], 0, key[1])] for key in FFN_ORDER}

                    def gather_down(c):
                        make_lo(at[("down", c)] + 1)
                        for m in range(KD):
                            if m == 3:
                                make_lo(at[("down", c)] + 2)
                            i = KD * c + m
                            dve.wait_ge(d_mm.sem, i + 1)
                            b = bank[5 + i % 3][:, 0:T]
                            if c == 0:
                                dve.tensor_copy(accT[:, m, :], b).then_inc(d_read.sem, 1)
                            else:
                                dve.wait_ge(d_read.sem, i - KD + 1)
                                dve.tensor_tensor(accT[:, m, :], accT[:, m, :], b, ALU.add).then_inc(d_read.sem, 1)

                    for c in range(NFC):
                        if c:
                            gather_down(c - 1)
                        make_lo(at[("up", c)] + 2)
                        for m in range(2):
                            dve.wait_ge(u_mm.sem, u_mm.at(c, m))
                            dve.wait_ge(g_read.sem, g_read.at(c, m))
                            if c:
                                dve.wait_ge(a_lo.sem, a_lo.at(c - 1))
                            dve.tensor_tensor(aa[:, m * T:(m + 1) * T], sil[:, m * T:(m + 1) * T], bank[3 + m][:, 0:T],
                                              ALU.mult).then_inc(a_ready.sem, 1)
                        dve.wait_ge(a_hi.sem, a_hi.at(c))
                        dve.tensor_tensor(dT_lo.rearrange("p j t -> p (j t)"), aa[:, :],
                                          dT_hi.rearrange("p j t -> p (j t)").bitcast(F32), ALU.subtract).then_inc(a_lo.sem, 1)
                    gather_down(NFC - 1)
                    dve.wait_ge(d_read.sem, KD * NFC)
                    add_channels(l)
                    modulation(1, 1)
                    layer_norm(l, 1)

            dve.wait_ge(rt_mm.sem, 1)
            link(dve.memset(lg[:], 0.0))
            for t, t0, n in VTILES:
                last = dve.tensor_copy(lg[0:n, 0, t, :], bank[5][0:n, t * NE:(t + 1) * NE])
            link(last)
            over_e = lambda r: red[:, r, :].unsqueeze(2).to_broadcast([P, NT, NE])
            link(dve.tensor_reduce(red[:, 0, :], lg[:, 0], AX.X, ALU.max))
            dve.tensor_tensor(lg[:, 1], lg[:, 0], over_e(0), ALU.subtract).then_inc(rt_sub.sem, 1)
            for i, (t, half) in enumerate((t, half) for t in range(NT) for half in range(2)):
                n = TILES[t][1]
                cols = slice(512 * half, 512 * half + 512)
                dve.wait_ge(h2_hi.sem, i + 1)
                dve.tensor_tensor(tok_lo[0:n, t, cols], bank[1 + i % 4][0:n, :], tok_hi[0:n, t, cols].bitcast(F32),
                                  ALU.subtract).then_inc(h2_lo.sem, 1)
            dve.wait_ge(rt_exp.sem, 1)
            link(dve.tensor_reduce(red[:, 1, :], lg[:, 1], AX.X, ALU.add))
            link(dve.reciprocal(red[:, 2, :], red[:, 1, :]))
            link(dve.tensor_tensor(lg[:, 1], lg[:, 1], over_e(2), ALU.mult))
            for t in range(NT):
                mine = lg[:, 1, t, :].unsqueeze(2).to_broadcast([P, NE, NE])
                other = lg[:, 1, t, :].unsqueeze(1).to_broadcast([P, NE, NE])
                dve.tensor_tensor(cmp[:, 0, t], other, mine, ALU.is_gt)
                link(dve.tensor_tensor(cmp[:, 1, t], other, mine, ALU.is_equal))
                link(dve.tensor_tensor(cmp[:, 1, t], cmp[:, 1, t], lower_e[:], ALU.mult))
                link(dve.tensor_tensor(cmp[:, 0, t], cmp[:, 0, t], cmp[:, 1, t], ALU.add))
                link(dve.tensor_reduce(lg[:, 2, t, :], cmp[:, 0, t], AX.X, ALU.add))
            dve.tensor_scalar(sel, lg[:, 2], TOP_K - 0.5, None, ALU.is_lt).then_inc(sel_ready.sem, 1)
            dve.wait_ge(sel_ready.sem, 1)
            link(dve.tensor_tensor(lg[:, 4], lg[:, 1], sel, ALU.mult))
            link(dve.tensor_reduce(red[:, 3, :], lg[:, 4], AX.X, ALU.add))
            link(dve.reciprocal(red[:, 4, :], red[:, 3, :]))
            link(dve.tensor_tensor(comb, lg[:, 4], over_e(4), ALU.mult))
            dve.wait_ge(pos_mm.sem, 1)
            link(dve.tensor_copy(cnt[:, 0:NE], bank[6][:, NT * NE:(NT + 1) * NE]))
            link(dve.tensor_reduce(cnt[:, 8:9], cnt[:, 0:NE], AX.X, ALU.max))
            link(dve.tensor_scalar(cnt[:, 9:10], cnt[:, 8:9], P + 0.5, 1.0, ALU.is_gt, ALU.add))
            link(dve.tensor_scalar(cnt[:, 10:11], cnt[:, 8:9], 2 * P + 0.5, None, ALU.is_gt))
            link(dve.tensor_tensor(cnt[:, 11:12], cnt[:, 9:10], cnt[:, 10:11], ALU.add))
            dve.tensor_copy(rounds_i[:], cnt[:, 11:12]).then_inc(rounds_ready.sem, 1)
            for t, t0, n in VTILES:
                last = dve.scalar_tensor_tensor(posm[0:n, t, :], bank[6][0:n, t * NE:(t + 1) * NE], 1.0, sel[0:n, t, :],
                                                ALU.add, ALU.mult)
            link(last)
            for t, t0, n in VTILES:
                last = dve.tensor_scalar(posm[0:n, t, :], posm[0:n, t, :], -1.0, None, ALU.add)
            link(last)
            dve.memset(accT[:], 0.0).then_inc(sc_read.sem, 1)
            dve.wait_ge(rounds_ready.sem, 1)
            rounds = dve.value_load(rounds_i[0:1, 0:1], min_val=1, max_val=NT)
            with dve.Fori(0, rounds) as rd:
                dve.wait_ge(sc_read.sem, rd * (NE * KD) + 1)
                for e in range(NE):
                    for t, t0, n in VTILES:
                        last = dve.tensor_scalar(G[0:n, t, e, :], col_iota[0:n, :], posm[0:n, t, e:e + 1], None, ALU.is_equal)
                last.then_inc(G_ready.sem, 1)
                dve.wait_ge(G_ready.sem, G_ready.at(rd))
                for t, t0, n in VTILES:
                    last = dve.tensor_scalar(posm[0:n, t, :], posm[0:n, t, :], -float(P), None, ALU.add)
                def expert_lo(it, first, upto):
                    for j in range(first, upto + 1):
                        s = moe_raw(j)[0]
                        dve.wait_ge(hi_ready.sem, it * NMC + (NSPLIT + j + 1))
                        dve.tensor_tensor(w_lo[:, (NSPLIT + j) % SPL, :], raw[:, s, :],
                                          w_hi[:, (NSPLIT + j) % SPL, :].bitcast(F32), ALU.subtract).then_inc(lo_ready.sem, 1)

                def tokens(it):
                    for half in range(2):
                        dve.wait_ge(xg_hi_ready.sem, xg_hi_ready.at(it, half))
                        ks = slice(4 * half, 4 * half + 4)
                        dve.tensor_tensor(xg_lo[:, ks, :].rearrange("p k s -> p (k s)"), bank[GX_BANKS[half]][:, :],
                                          xg_hi[:, ks, :].rearrange("p k s -> p (k s)").bitcast(F32),
                                          ALU.subtract).then_inc(xg_lo_ready.sem, 1)

                def gated(it, c):
                    dve.wait_ge(eu_mm.sem, eu_mm.at(it, c))
                    dve.wait_ge(eg_read.sem, eg_read.at(it, c))
                    if c >= 2:
                        dve.wait_ge(eT_mm.sem, eT_mm.at(it, c - 2))
                    cs = slice(c % 2 * CW, (c % 2 + 1) * CW)
                    dve.tensor_tensor(aa[:, cs], sil[:, cs], bank[3 + c % 2][:, 0:CW], ALU.mult).then_inc(ea_ready.sem, 1)

                def turned(it, c):
                    dve.wait_ge(ea_hi.sem, ea_hi.at(it, c))
                    dve.tensor_tensor(aT_lo.rearrange("p j s -> p (j s)"), bank[7][:, 0:CW],
                                      aT_hi.rearrange("p j s -> p (j s)").bitcast(F32), ALU.subtract).then_inc(ea_lo.sem, 1)

                def expert(it, following):
                    gated(it, 0)
                    for c in range(NFC - 1):
                        expert_lo(it, 3 * c + 3, 3 * c + 4)
                        turned(it, c)
                        expert_lo(it, 3 * c + 5, min(3 * c + 5, NMC - 1))
                        gated(it, c + 1)
                    if following is not None:
                        expert_lo(following, 0, 0)
                    turned(it, NFC - 1)
                    if following is not None:
                        expert_lo(following, 1, 1)
                        tokens(following)
                    dve.wait_ge(ed_mm.sem, ed_mm.at(it, NFC - 1))

                def add_up(it, e, following):
                    col = slice(e, e + 1) if isinstance(e, int) else bass.ds(e, 1)
                    for half in range(2):
                        dve.tensor_scalar(yf[:, 512 * half:512 * half + 512], bank[5 + half][:, :], wslot[:, col],
                                          None, ALU.mult).then_inc(y_read.sem, 1)
                    for half in range(2):
                        cols = slice(512 * half, 512 * half + 512)
                        dve.wait_ge(yw_hi.sem, yw_hi.at(it, half))
                        dve.tensor_tensor(y_lo[:, cols], yf[:, cols], y_hi[:, cols].bitcast(F32), ALU.subtract).then_inc(yw_lo.sem, 1)
                    for m in range(KD):
                        if m == 4 and following is not None:
                            expert_lo(following, 2, 2)
                        dve.wait_ge(sc_mm.sem, sc_mm.at(it, m))
                        dve.tensor_tensor(accT[:, m, :], accT[:, m, :], bank[SC_BANKS[m % 4]][:, 0:T], ALU.add).then_inc(sc_read.sem, 1)

                first = dve.snap(rd * NE)
                expert_lo(first, 0, 0)
                tokens(first)
                dve.wait_ge(wsl_mm.sem, wsl_mm.at(rd))
                dve.tensor_copy(wslot[:], bank[5][:, 0:NE]).then_inc(wsl_ready.sem, 1)
                dve.wait_ge(wsl_ready.sem, wsl_ready.at(rd))
                expert_lo(first, 1, SPL - 1)
                with dve.Fori(0, NE - 1) as e:
                    it = dve.snap(rd * NE + e)
                    following = dve.snap(rd * NE + e + 1)
                    expert(it, following)
                    add_up(it, e, following)
                it = dve.snap(rd * NE + (NE - 1))
                expert(it, None)
                add_up(it, NE - 1, None)
            dve.wait_ge(sc_read.sem, rounds * (NE * KD) + 1)
            add_channels(DEPTH - 1)
            layer_norm(DEPTH - 1, 1)


_INS = ['x_prompt', 'x_sample', 'state_hgrn', 'c_prompt', 'c_sample', 'w_ada', 'b_ada', 'w_in', 'w_out', 'a_ln_w', 'a_ln_b',
        'a_ws', 'a_bs', 'lb_logits', 'b_norm_w', 'ln1_w', 'ln1_b', 'ln2_w', 'ln2_b', 'w_ff_gate', 'w_ff_up', 'w_ff_down',
        'w_router', 'e_gate', 'e_up', 'e_down']
_OUTS = [((1, 256, 1024), 'float32'), ((8, 8, 1024), 'float32'), ((2, 1, 4, 128, 128), 'float32'),
         ((2, 8, 4, 128, 128), 'float32'), ((2, 1, 128, 512), 'float32'), ((2, 8, 8, 512), 'float32')]


def kernel(**inputs):
    import numpy as _np
    import concourse.bacc as _bacc
    from concourse import mybir as _mybir
    from concourse.bass_utils import run_bass_kernel_spmd as _run

    nc = _bacc.Bacc("TRN2", target_bir_lowering=False, num_devices=1)
    arrays, args = {}, []
    for name in _INS:
        a = _np.ascontiguousarray(inputs[name])
        arrays[f"in_{name}_dram"] = a
        args.append(nc.dram_tensor(f"in_{name}_dram", a.shape, _mybir.dt.from_np(a.dtype), kind="ExternalInput").ap())
    for i, (shape, dtype) in enumerate(_OUTS):
        dt = _mybir.dt.from_np(_np.dtype(dtype))
        args.append(nc.dram_tensor(f"out_{i}_dram", shape, dt, kind="ExternalOutput").ap())
    hybrid_trunk(nc, *args)
    r = _run(nc, [arrays], core_ids=[0])
    return tuple(r.results[0][f"out_{i}_dram"] for i in range(len(_OUTS)))
```
